# Optimizing a Trainium2 kernel written in Bass

```python
import math
import jax, jax.numpy as jnp
from jax import lax
import numpy as np

D_MODEL = 1024
BATCH = 1
SEQ = 2048
DEPTH = 2

CTX_LEN = 256
GRID_W = 64
EPS = 1e-6
N_DIR = 2

W_BRANCH = D_MODEL // 4
D_MIX = 4 * W_BRANCH

ML_HEADS = 4
ML_DH = W_BRANCH // ML_HEADS
ML_CHUNK = 128

DA_HEADS = 4
DA_V = W_BRANCH // DA_HEADS
DA_QK = DA_V // 2
Q_BLOCK = 128
ROPE_BASE = 10000.0
ROPE_AXIS = DA_QK // 2

SSM_HEADS = 4
SSM_P = W_BRANCH // SSM_HEADS
SSM_D_INNER = SSM_HEADS * SSM_P
SSM_GROUPS = 2
SSM_N = 128
SSM_CONV = 3
SSM_CHUNK = 128
SSM_XBC = SSM_D_INNER + 2 * SSM_GROUPS * SSM_N

HG_HEADS = 4
HG_DK = W_BRANCH // HG_HEADS
HG_DV = W_BRANCH // HG_HEADS
HG_CHUNK = 16

SEGMENTS = (
    ("ml_q", ML_HEADS * ML_DH), ("ml_k", ML_HEADS * ML_DH), ("ml_v", ML_HEADS * ML_DH),
    ("ml_o", ML_HEADS * ML_DH), ("ml_i", N_DIR * ML_HEADS), ("ml_f", N_DIR * ML_HEADS), ("ml_z", W_BRANCH),
    ("da_q", DA_HEADS * 2 * DA_QK), ("da_k", DA_HEADS * 2 * DA_QK), ("da_v", DA_HEADS * DA_V), ("da_z", W_BRANCH),
    ("ss_xbc", SSM_XBC), ("ss_dt", N_DIR * SSM_HEADS), ("ss_z", W_BRANCH),
    ("hg_q", HG_HEADS * HG_DK), ("hg_f", N_DIR * HG_HEADS * HG_DK), ("hg_i", HG_HEADS * HG_DV), ("hg_z", W_BRANCH),
)
D_IN = sum(n for _, n in SEGMENTS)

kernel_name = "hybrid_mlstm_diffattn_ssd_hgrn2_prefix_dit"

F32 = jnp.float32

def rmsnorm(x, g):
    xf = x.astype(F32)
    y = xf * lax.rsqrt(jnp.mean(xf * xf, axis=-1, keepdims=True) + EPS)
    return (y * g).astype(x.dtype)

def head_layernorm(x, g):
    xf = x.astype(F32)
    mu = jnp.mean(xf, axis=-1, keepdims=True)
    var = jnp.mean(jnp.square(xf - mu), axis=-1, keepdims=True)
    return (xf - mu) * lax.rsqrt(var + EPS) * g

def split_cols(u):
    out, off = {}, 0
    for name, n in SEGMENTS:
        out[name] = u[..., off:off + n]
        off += n
    return out

def axial_rope(n_rows):
    rows = jnp.repeat(jnp.arange(n_rows), GRID_W).astype(F32)
    cols = (jnp.arange(n_rows * GRID_W) % GRID_W).astype(F32)
    inv = ROPE_BASE ** (-jnp.arange(0, ROPE_AXIS, 2, dtype=F32) / ROPE_AXIS)
    ang = jnp.concatenate([rows[:, None] * inv, cols[:, None] * inv], axis=-1)
    return jnp.cos(ang), jnp.sin(ang)

def apply_rope(x, cos, sin):
    half = x.shape[-1] // 2
    x1, x2 = x[..., :half], x[..., half:]
    cos = cos[None, :, None, None, :]
    sin = sin[None, :, None, None, :]
    return jnp.concatenate([x1 * cos - x2 * sin, x1 * sin + x2 * cos], axis=-1)

def dwconv_centred(x, w, b):
    k = w.shape[0]
    y = lax.conv_general_dilated(x, w[:, None, :].astype(x.dtype), window_strides=(1,),
                                 padding=[((k - 1) // 2, k // 2)],
                                 dimension_numbers=("NWC", "WIO", "NWC"),
                                 feature_group_count=x.shape[-1])
    return y + b

def chunk_state_scan(decay, incr, s0):
    def step(s, inp):
        d, u = inp
        return d * s + u, s
    final, starts = lax.scan(step, s0, (jnp.moveaxis(decay, 1, 0), jnp.moveaxis(incr, 1, 0)))
    return jnp.moveaxis(starts, 0, 1), final

def bidirectional(run, ctx_fwd, lat_fwd, ctx_bwd, lat_bwd, s0, ctx_out):
    flip = lambda args: tuple(jnp.flip(a, axis=1) for a in args)
    yc_f, sc_f = run(ctx_fwd, s0, ctx_out)
    yl_f, _ = run(lat_fwd, sc_f, True)
    yc_b, sc_b = run(flip(ctx_bwd), s0, ctx_out)
    yl_b, _ = run(flip(lat_bwd), sc_b, True)
    y_lat = yl_f + jnp.flip(yl_b, axis=1)
    y_ctx = yc_f + jnp.flip(yc_b, axis=1) if ctx_out else None
    return y_lat, y_ctx

def mlstm_run(args, state, with_out):
    q, k, v, li, lf = args
    bsz, t, h, d = q.shape
    L = ML_CHUNK
    nc = t // L
    r = lambda a: a.reshape(bsz, nc, L, *a.shape[2:])
    q, k, v, li, lf = (r(a) for a in (q, k, v, li, lf))
    F = jnp.cumsum(lf, axis=2)
    FL = F[:, :, -1]
    w_end = FL[:, :, None] - F + li
    b_end = jnp.max(w_end, axis=2)
    e = jnp.exp(w_end - b_end[:, :, None])
    dC = jnp.einsum('bclh,bclhk,bclhv->bchkv', e, k, v)
    dn = jnp.einsum('bclh,bclhk->bchk', e, k)

    def step(carry, inp):
        C, n, m = carry
        fl, bb, dc, dnn = inp
        m_new = jnp.maximum(fl + m, bb)
        a = jnp.exp(fl + m - m_new)
        g = jnp.exp(bb - m_new)
        return (a[..., None, None] * C + g[..., None, None] * dc, a[..., None] * n + g[..., None] * dnn, m_new), (C, n, m)

    tm = lambda a: jnp.moveaxis(a, 1, 0)
    final, (Cs, ns, ms) = lax.scan(step, state, (tm(FL), tm(b_end), tm(dC), tm(dn)))
    if not with_out:
        return None, final
    Cs, ns, ms = tm(Cs), tm(ns), tm(ms)
    mask = jnp.tril(jnp.ones((L, L), bool))
    Dm = jnp.where(mask[:, :, None], F[:, :, :, None, :] - F[:, :, None, :, :] + li[:, :, None, :, :], -jnp.inf)
    a_int = F + ms[:, :, None, :]
    m_i = jnp.maximum(a_int, jnp.max(Dm, axis=3))
    P = jnp.exp(Dm - m_i[:, :, :, None, :])
    s = jnp.einsum('bcihd,bcjhd->bcijh', q, k) * P
    w_int = jnp.exp(a_int - m_i)
    num = jnp.einsum('bcijh,bcjhv->bcihv', s, v) + w_int[..., None] * jnp.einsum('bcihk,bchkv->bcihv', q, Cs)
    den = jnp.sum(s, axis=3) + w_int * jnp.einsum('bcihk,bchk->bcih', q, ns)
    hh = num / jnp.maximum(jnp.abs(den), jnp.exp(-m_i))[..., None]
    return hh.reshape(bsz, t, h, d), final

def mlstm_branch(s_lat, s_ctx, gate_b, norm_g, ctx_out):
    def prep(s):
        bsz, t, _ = s["ml_q"].shape
        heads = lambda a: a.reshape(bsz, t, ML_HEADS, ML_DH)
        q, k, v = heads(s["ml_q"]), heads(s["ml_k"]) * (ML_DH ** -0.5), heads(s["ml_v"])
        ig = s["ml_i"].reshape(bsz, t, N_DIR, ML_HEADS).astype(F32) + gate_b[:, 0]
        lf = jax.nn.log_sigmoid(s["ml_f"].reshape(bsz, t, N_DIR, ML_HEADS).astype(F32) + gate_b[:, 1])
        return (q, k, v, ig[:, :, 0], lf[:, :, 0]), (q, k, v, ig[:, :, 1], lf[:, :, 1])
    lat_f, lat_b = prep(s_lat)
    ctx_f, ctx_b = prep(s_ctx)
    bsz = s_lat["ml_q"].shape[0]
    s0 = (jnp.zeros((bsz, ML_HEADS, ML_DH, ML_DH), F32), jnp.zeros((bsz, ML_HEADS, ML_DH), F32),
          jnp.zeros((bsz, ML_HEADS), F32))
    h_lat, h_ctx = bidirectional(mlstm_run, ctx_f, lat_f, ctx_b, lat_b, s0, ctx_out)

    def finish(hh, s):
        o = jax.nn.sigmoid(s["ml_o"].astype(F32)).reshape(hh.shape)
        y = head_layernorm(o * hh, norm_g.reshape(ML_HEADS, ML_DH))
        return y.reshape(*y.shape[:2], -1) * jax.nn.silu(s["ml_z"])
    return finish(h_lat, s_lat), (finish(h_ctx, s_ctx) if ctx_out else None)

def diff_attend(q, k, v, lam):
    s = jnp.einsum('bqhmd,bkhmd->bhmqk', q, k).astype(F32) * (DA_QK ** -0.5)
    p = jax.nn.softmax(s, axis=-1)
    w = p[:, :, 0] - lam * p[:, :, 1]
    return jnp.einsum('bhqk,bkhv->bqhv', w, v)

def diff_attn_branch(s_lat, s_ctx, lam_vecs, norm_g, lam_init, rope_cos, rope_sin, ctx_out):
    def prep(s):
        bsz, t, _ = s["da_q"].shape
        q = s["da_q"].reshape(bsz, t, DA_HEADS, 2, DA_QK)
        k = s["da_k"].reshape(bsz, t, DA_HEADS, 2, DA_QK)
        v = s["da_v"].reshape(bsz, t, DA_HEADS, DA_V)
        return q, k, v
    ql, kl, vl = prep(s_lat)
    qc, kc, vc = prep(s_ctx)
    lv = lam_vecs.astype(F32)
    lam = jnp.exp(jnp.sum(lv[0] * lv[1])) - jnp.exp(jnp.sum(lv[2] * lv[3])) + lam_init
    ql = apply_rope(ql, rope_cos, rope_sin)
    kl = apply_rope(kl, rope_cos, rope_sin)
    k_all = jnp.concatenate([kl, kc], axis=1)
    v_all = jnp.concatenate([vl, vc], axis=1)
    bsz, t = ql.shape[:2]
    n_blk = t // Q_BLOCK
    q_blocks = jnp.moveaxis(ql.reshape(bsz, n_blk, Q_BLOCK, DA_HEADS, 2, DA_QK), 1, 0)
    o_lat = lax.map(lambda qb: diff_attend(qb, k_all, v_all, lam), q_blocks)
    o_lat = jnp.moveaxis(o_lat, 0, 1).reshape(bsz, t, DA_HEADS, DA_V)

    def finish(o, s):
        o = rmsnorm(o, norm_g) * (1.0 - lam_init)
        return o.reshape(*o.shape[:2], -1) * jax.nn.silu(s["da_z"])
    y_ctx = finish(diff_attend(qc, kc, vc, lam), s_ctx) if ctx_out else None
    return finish(o_lat, s_lat), y_ctx

def ssd_run(args, s0, with_out):
    xh, dt, a, Bh, Ch = args
    bsz, t, h, p = xh.shape
    L = SSM_CHUNK
    nc = t // L
    r = lambda z: z.reshape(bsz, nc, L, *z.shape[2:])
    xh, dt, a, Bh, Ch = (r(z) for z in (xh, dt, a, Bh, Ch))
    Acum = jnp.cumsum(a, axis=2)
    AL = Acum[:, :, -1]
    dS = jnp.einsum('bclh,bclhn,bclhp->bchnp', jnp.exp(AL[:, :, None] - Acum) * dt, Bh, xh)
    starts, final = chunk_state_scan(jnp.exp(AL)[..., None, None], dS, s0)
    if not with_out:
        return None, final
    mask = jnp.tril(jnp.ones((L, L), bool))
    Lm = jnp.exp(jnp.where(mask[:, :, None], Acum[:, :, :, None, :] - Acum[:, :, None, :, :], -jnp.inf))
    sc = jnp.einsum('bcihn,bcjhn->bcijh', Ch, Bh) * Lm * dt[:, :, None]
    y = jnp.einsum('bcijh,bcjhp->bcihp', sc, xh) + jnp.exp(Acum)[..., None] * jnp.einsum('bcihn,bchnp->bcihp', Ch, starts)
    return y.reshape(bsz, t, h, p), final

def ssd_branch(s_lat, s_ctx, conv_w, conv_b, dt_bias, a_log, d_skip, norm_g, ctx_out):
    A = -jnp.exp(a_log.astype(F32))
    rep = SSM_HEADS // SSM_GROUPS

    def prep(s):
        xbc = jax.nn.silu(dwconv_centred(s["ss_xbc"], conv_w, conv_b))
        bsz, t, _ = xbc.shape
        xh = xbc[..., :SSM_D_INNER].reshape(bsz, t, SSM_HEADS, SSM_P)
        Bm = xbc[..., SSM_D_INNER:SSM_D_INNER + SSM_GROUPS * SSM_N].reshape(bsz, t, SSM_GROUPS, SSM_N)
        Cm = xbc[..., SSM_D_INNER + SSM_GROUPS * SSM_N:].reshape(bsz, t, SSM_GROUPS, SSM_N)
        Bh = jnp.repeat(Bm, rep, axis=2)
        Ch = jnp.repeat(Cm, rep, axis=2)
        dt = jax.nn.softplus(s["ss_dt"].reshape(bsz, t, N_DIR, SSM_HEADS).astype(F32) + dt_bias)
        fwd = (xh, dt[:, :, 0], dt[:, :, 0] * A[0], Bh, Ch)
        bwd = (xh, dt[:, :, 1], dt[:, :, 1] * A[1], Bh, Ch)
        return fwd, bwd, xh
    lat_f, lat_b, xl = prep(s_lat)
    ctx_f, ctx_b, xc = prep(s_ctx)
    bsz = xl.shape[0]
    s0 = jnp.zeros((bsz, SSM_HEADS, SSM_N, SSM_P), F32)
    y_lat, y_ctx = bidirectional(ssd_run, ctx_f, lat_f, ctx_b, lat_b, s0, ctx_out)

    def finish(y, xh, s):
        y = y + d_skip[:, None] * xh
        bs, t = y.shape[:2]
        y = y.reshape(bs, t, SSM_D_INNER) * jax.nn.silu(s["ss_z"])
        y = rmsnorm(y.reshape(bs, t, SSM_GROUPS, SSM_D_INNER // SSM_GROUPS), norm_g.reshape(SSM_GROUPS, -1))
        return y.reshape(bs, t, SSM_D_INNER)
    return finish(y_lat, xl, s_lat), (finish(y_ctx, xc, s_ctx) if ctx_out else None)

def hgrn2_run(args, s0, with_out):
    q, lg, kk, v = args
    bsz, t, h, dk = q.shape
    L = HG_CHUNK
    nc = t // L
    r = lambda z: z.reshape(bsz, nc, L, *z.shape[2:])
    q, lg, kk, v = (r(z) for z in (q, lg, kk, v))
    G = jnp.cumsum(lg, axis=2)
    GL = G[:, :, -1]
    dS = jnp.einsum('bclhk,bclhv->bchkv', kk * jnp.exp(GL[:, :, None] - G), v)
    starts, final = chunk_state_scan(jnp.exp(GL)[..., None], dS, s0)
    if not with_out:
        return None, final
    mask = jnp.tril(jnp.ones((L, L), bool))
    dec = jnp.exp(jnp.where(mask[:, :, None, None], G[:, :, :, None] - G[:, :, None, :], -jnp.inf))
    Aw = jnp.einsum('bcihk,bcjhk,bcijhk->bcijh', q, kk, dec)
    o = jnp.einsum('bcijh,bcjhv->bcihv', Aw, v) + jnp.einsum('bcihk,bchkv->bcihv', q * jnp.exp(G), starts)
    return o.reshape(bsz, t, h, -1), final

def hgrn2_branch(s_lat, s_ctx, lb, norm_g, ctx_out):
    lbh = lb.astype(F32).reshape(N_DIR, HG_HEADS, HG_DK)
    log_lb, log_1mlb = jnp.log(lbh), jnp.log1p(-lbh)

    def prep(s):
        bsz, t, _ = s["hg_q"].shape
        q = jax.nn.silu(s["hg_q"]).reshape(bsz, t, HG_HEADS, HG_DK)
        z = s["hg_f"].reshape(bsz, t, N_DIR, HG_HEADS, HG_DK).astype(F32)
        logf = jnp.logaddexp(log_lb, log_1mlb + jax.nn.log_sigmoid(z))
        kk = (1.0 - lbh) * jax.nn.sigmoid(-z)
        v = s["hg_i"].reshape(bsz, t, HG_HEADS, HG_DV)
        return (q, logf[:, :, 0], kk[:, :, 0], v), (q, logf[:, :, 1], kk[:, :, 1], v)
    lat_f, lat_b = prep(s_lat)
    ctx_f, ctx_b = prep(s_ctx)
    bsz = s_lat["hg_q"].shape[0]
    s0 = jnp.zeros((bsz, HG_HEADS, HG_DK, HG_DV), F32)
    o_lat, o_ctx = bidirectional(hgrn2_run, ctx_f, lat_f, ctx_b, lat_b, s0, ctx_out)

    def finish(o, s):
        o = rmsnorm(o, norm_g.reshape(HG_HEADS, HG_DV))
        return o.reshape(*o.shape[:2], -1) * jax.nn.silu(s["hg_z"])
    return finish(o_lat, s_lat), (finish(o_ctx, s_ctx) if ctx_out else None)

def hybrid_layer(x, ctx, c, c_ctx, w_mod, b_mod, norm_g, w_in, w_out,
                 ml_gate_b, ml_norm_g, da_lambda, da_norm_g,
                 ss_conv_w, ss_conv_b, ss_dt_bias, ss_a_log, ss_d, ss_norm_g,
                 hg_lb, hg_norm_g, lam_init, rope_cos, rope_sin, ctx_out):
    shift, scale, gate = jnp.split(jax.nn.silu(c) @ w_mod + b_mod, 3, axis=-1)
    shift_c, scale_c, gate_c = jnp.split(jax.nn.silu(c_ctx) @ w_mod + b_mod, 3, axis=-1)
    h_lat = rmsnorm(x, norm_g) * (1.0 + scale[:, None]) + shift[:, None]
    h_ctx = rmsnorm(ctx, norm_g) * (1.0 + scale_c) + shift_c
    s_lat = split_cols(h_lat @ w_in)
    s_ctx = split_cols(h_ctx @ w_in)
    branches = (
        mlstm_branch(s_lat, s_ctx, ml_gate_b, ml_norm_g, ctx_out),
        diff_attn_branch(s_lat, s_ctx, da_lambda, da_norm_g, lam_init, rope_cos, rope_sin, ctx_out),
        ssd_branch(s_lat, s_ctx, ss_conv_w, ss_conv_b, ss_dt_bias, ss_a_log, ss_d, ss_norm_g, ctx_out),
        hgrn2_branch(s_lat, s_ctx, hg_lb, hg_norm_g, ctx_out),
    )
    y_lat = jnp.concatenate([br[0] for br in branches], axis=-1) @ w_out
    x = x + gate[:, None] * y_lat
    if ctx_out:
        y_ctx = jnp.concatenate([br[1] for br in branches], axis=-1) @ w_out
        ctx = ctx + gate_c * y_ctx
    return x, ctx

def setup_inputs(seed: int = 0) -> dict:
    key = jax.random.key(seed)
    ks = jax.random.split(key, 24)
    nrm = lambda k, shape, s: jax.random.normal(k, shape, F32) * s
    x = nrm(ks[0], (BATCH, SEQ, D_MODEL), 1.0)
    c = nrm(ks[1], (BATCH, D_MODEL), 1.0)
    ctx = nrm(ks[2], (BATCH, CTX_LEN, D_MODEL), 1.0)
    c_ctx = nrm(ks[3], (D_MODEL,), 1.0)
    w_mod = nrm(ks[4], (DEPTH, D_MODEL, 3 * D_MODEL), 0.5 * D_MODEL ** -0.5)
    b_mod = nrm(ks[5], (DEPTH, 3 * D_MODEL), 0.02)
    norm_g = 1.0 + nrm(ks[6], (DEPTH, D_MODEL), 0.02)
    w_in = nrm(ks[7], (DEPTH, D_MODEL, D_IN), D_MODEL ** -0.5)
    w_out = nrm(ks[8], (DEPTH, D_MIX, D_MODEL), D_MIX ** -0.5)
    f_bias = jnp.linspace(3.0, 6.0, ML_HEADS, dtype=F32)
    ml_gate_b = jnp.stack([nrm(ks[9], (DEPTH, N_DIR, ML_HEADS), 0.1),
                           f_bias + nrm(ks[10], (DEPTH, N_DIR, ML_HEADS), 0.1)], axis=2)
    ml_norm_g = 1.0 + nrm(ks[11], (DEPTH, W_BRANCH), 0.02)
    da_lambda = nrm(ks[12], (DEPTH, 4, DA_QK), 0.1)
    da_norm_g = 1.0 + nrm(ks[13], (DEPTH, DA_V), 0.02)
    ss_conv_w = nrm(ks[14], (DEPTH, SSM_CONV, SSM_XBC), SSM_CONV ** -0.5)
    ss_conv_b = nrm(ks[15], (DEPTH, SSM_XBC), 0.02)
    dt0 = jnp.exp(jax.random.uniform(ks[16], (DEPTH, N_DIR, SSM_HEADS), F32, math.log(1e-3), math.log(1e-1)))
    ss_dt_bias = dt0 + jnp.log(-jnp.expm1(-dt0))
    ss_a_log = jnp.log(jax.random.uniform(ks[17], (DEPTH, N_DIR, SSM_HEADS), F32, 1.0, 16.0))
    ss_d = 1.0 + nrm(ks[18], (DEPTH, SSM_HEADS), 0.1)
    ss_norm_g = 1.0 + nrm(ks[19], (DEPTH, W_BRANCH), 0.02)
    hg_lower = nrm(ks[20], (N_DIR, DEPTH, HG_HEADS * HG_DK), 1.0)
    hg_norm_g = 1.0 + nrm(ks[21], (DEPTH, W_BRANCH), 0.02)
    final_g = 1.0 + nrm(ks[22], (D_MODEL,), 0.02)
    return {"x": x, "c": c, "ctx": ctx, "c_ctx": c_ctx, "w_mod": w_mod, "b_mod": b_mod,
            "norm_g": norm_g, "w_in": w_in, "w_out": w_out, "ml_gate_b": ml_gate_b,
            "ml_norm_g": ml_norm_g, "da_lambda": da_lambda, "da_norm_g": da_norm_g,
            "ss_conv_w": ss_conv_w, "ss_conv_b": ss_conv_b, "ss_dt_bias": ss_dt_bias,
            "ss_a_log": ss_a_log, "ss_d": ss_d, "ss_norm_g": ss_norm_g, "hg_lower": hg_lower,
            "hg_norm_g": hg_norm_g, "final_g": final_g}

def reference(x, c, ctx, c_ctx, w_mod, b_mod, norm_g, w_in, w_out, ml_gate_b, ml_norm_g,
              da_lambda, da_norm_g, ss_conv_w, ss_conv_b, ss_dt_bias, ss_a_log, ss_d, ss_norm_g,
              hg_lower, hg_norm_g, final_g):
    n_rows = x.shape[1] // GRID_W
    rope_cos, rope_sin = axial_rope(n_rows)
    lb_all = jnp.cumsum(jax.nn.softmax(hg_lower.astype(F32), axis=1), axis=1)
    lb_all = lb_all - lb_all[:, :1]
    for l in range(DEPTH):
        lam_init = 0.8 - 0.6 * math.exp(-0.3 * l)
        x, ctx = hybrid_layer(x, ctx, c, c_ctx, w_mod[l], b_mod[l], norm_g[l], w_in[l], w_out[l],
                              ml_gate_b[l], ml_norm_g[l], da_lambda[l], da_norm_g[l],
                              ss_conv_w[l], ss_conv_b[l], ss_dt_bias[l], ss_a_log[l], ss_d[l], ss_norm_g[l],
                              lb_all[:, l], hg_norm_g[l], lam_init, rope_cos, rope_sin,
                              l < DEPTH - 1)
    return rmsnorm(x, final_g)


_drawn_inputs = setup_inputs


def setup_inputs(seed=0):
    import zlib

    import numpy as np

    out = dict(_drawn_inputs(seed))
    spreads = {}
    factors = {'ctx': 2.677,
     'norm_g': 4.939,
     'ml_norm_g': 8.0,
     'da_lambda': 7.159,
     'da_norm_g': 8.0,
     'ss_conv_b': 8.0,
     'ss_d': 200.0,
     'ss_norm_g': 28.31,
     'hg_lower': 5.526,
     'hg_norm_g': 8.0,
     'final_g': 20.714}
    for name, (base, spread) in spreads.items():
        noise = np.random.default_rng([zlib.crc32(name.encode()), seed]).standard_normal(out[name].shape)
        drawn = base * np.exp(spread * noise) if base else spread * noise
        out[name] = __import__('jax').numpy.asarray(drawn.astype(out[name].dtype))
    for name, factor in factors.items():
        out[name] = (out[name] * factor).astype(out[name].dtype)
    return out
```

```python
from contextlib import ExitStack
import math

import numpy as np
import concourse.bass as bass
from concourse import mybir

F32 = mybir.dt.float32
BF16 = mybir.dt.bfloat16
ALU = mybir.AluOpType
ACT = mybir.ActivationFunctionType
AX = mybir.AxisListType

P = 128
D = 1024
SEQ = 2048
CTX = 256
DEPTH = 2
KT = D // P
CT = CTX // P
NT = (SEQ + CTX) // P
EPS = 1e-6
H = 4
DH = 64
GRID_W = 64
ROPE_BASE = 10000.0
LEVELS = 7

_SEG = (("ml_q", 256), ("ml_k", 256), ("ml_v", 256), ("ml_o", 256), ("ml_i", 8), ("ml_f", 8), ("ml_z", 256),
        ("da_q", 256), ("da_k", 256), ("da_v", 256), ("da_z", 256),
        ("ss_xbc", 768), ("ss_dt", 8), ("ss_z", 256),
        ("hg_q", 256), ("hg_f", 512), ("hg_i", 256), ("hg_z", 256), ("hg_k", 512))
OFF = {}
_o = 0
for _n, _w in _SEG:
    OFF[_n] = _o
    _o += _w
UW = _o
DIN = OFF["hg_k"]
XBC = 768
BLOCKS = [(0, 512), (512, 512), (1024, 272), (1296, 512), (1808, 512), (2320, 512), (2832, 264),
          (3096, 512), (3608, 512), (4120, 512)]
BANKS = 8
GC = {n: 8 * i for i, n in enumerate(["lf", "wk", "wint", "em", "a", "dt", "ws", "ea", "cum", "as"])}
GW = 80
STW = 2 * 65 + 2 * 64 + 4 * 64
ST_ML, ST_HG, ST_SS = 0, 130, 258


def dram_constants():
    s = np.arange(P)
    le = (s[:, None] <= s[None, :]).astype(np.float32)
    lt = (s[:, None] < s[None, :]).astype(np.float32)
    tri = np.stack([le, le.T, lt.T, lt], 1)
    mats = np.zeros((P, 2 * LEVELS, P), np.float32)
    masks = np.zeros((P, 2 * (LEVELS + 1), P), np.float32)
    for lv in range(LEVELS):
        w = 1 << lv
        for t in range(P):
            mid = (t // (2 * w)) * 2 * w + w
            if t >= mid:
                mats[mid:t + 1, 2 * lv, t] = 1
                mats[mid:t, 2 * lv + 1, t] = 1
            else:
                mats[t + 1:mid, 2 * lv, t] = 1
                mats[t:mid, 2 * lv + 1, t] = 1
        same = (s[:, None] // (2 * w)) == (s[None, :] // (2 * w))
        right = (s // w) % 2 == 1
        masks[:, 2 * lv] = same & ~right[:, None] & right[None, :]
        masks[:, 2 * lv + 1] = same & right[:, None] & ~right[None, :]
    masks[:, 2 * LEVELS] = masks[:, 2 * LEVELS + 1] = np.eye(P)
    neg = np.zeros((P, 2, P), np.float32)
    neg[:, 0] = -1e30 * (s[:, None] > s[None, :])
    neg[:, 1] = -1e30 * (s[:, None] < s[None, :])
    sel = np.zeros((8, 8, P), np.float32)
    sel[np.arange(8), np.arange(8)] = 1
    pick = np.zeros((P, 2, P), np.float32)
    pick[P - 1, 0] = 1
    pick[0, 1] = 1
    pos = np.arange(SEQ)
    inv = ROPE_BASE ** (-np.arange(0, 16, 2, dtype=np.float32) / np.float32(16))
    ang = np.concatenate([(pos // GRID_W).astype(np.float32)[:, None] * inv,
                          (pos % GRID_W).astype(np.float32)[:, None] * inv], -1).astype(np.float32)
    rope = np.zeros((SEQ + CTX, 32), np.float32)
    rope[:CTX, :16] = 1
    rope[CTX:, :16] = np.cos(ang)
    rope[CTX:, 16:] = np.sin(ang)
    return {"c_ident": np.eye(P, dtype=np.float32), "c_tri": tri, "c_mats": mats, "c_masks": masks,
            "c_neg": neg, "c_sel": sel, "c_pick": pick, "c_rope": rope}


class Steps:

    def __init__(self, eng, sem):
        self.eng, self.sem, self.n = eng, sem, 0

    def mark(self, ins):
        self.n += 1
        ins.then_inc(self.sem, 1)
        return self.n

    def wait(self, n=None):
        self.eng.wait_ge(self.sem, self.n if n is None else n)

    def then(self, ins):
        self.mark(ins)
        self.wait()

    def clear(self):
        self.wait()
        self.eng.sem_clear(self.sem)
        self.n = 0


TABLES = "natural_log_exp_and_others"

SCRATCH = [("u", (NT, P, UW), np.float32),
           ("xbc", (NT + 2, P + 2, XBC), np.float32),
           ("xc", (NT, P, XBC), np.float32),
           ("gt", (NT, P, GW), np.float32),
           ("gr", (NT, 2, 8, P), np.float32),
           ("st", (NT, P, STW), np.float32),
           ("y", (NT, P, D), np.float32),
           ("stream", (NT, P, D), np.float32),
           ("modrow", (DEPTH, 2, 3 * D), np.float32),
           ("rows", (DEPTH, 2, 512), np.float32)]


class Kernel:
    def __init__(self, nc, ins, out, preset=()):
        self.preset = preset; self.nc, self.x, self.out, self.tag = nc, ins, out, "all"
        a = {name: nc.dram_tensor(name, shape, F32, kind="ExternalInput" if name in preset else "Internal").ap()
             for name, shape, _ in SCRATCH}
        self.u, self.xbc, self.xc, self.gt, self.gr = a["u"], a["xbc"], a["xc"], a["gt"], a["gr"]
        self.st, self.y, self.stream, self.modrow, self.rows = a["st"], a["y"], a["stream"], a["modrow"], a["rows"]

        self.qa, self.qb = [nc.dram_tensor(name, (NT, P, 2 * H * P), BF16, kind="Internal").ap() for name in ("qa", "qb")]
        self.rope = ins["c_rope"].rearrange("(t p) n -> t p n", p=P)

    def sb(self, c, name, shape, dt=F32):
        return c.enter_context(self.nc.sbuf_tensor(f"{self.tag}_{name}", shape, dt))

    def sem(self, c, name):
        return c.enter_context(self.nc.semaphore(f"{self.tag}_{name}"))

    def sems(self, c, names):
        return {n: self.sem(c, n) for n in names.split()}

    def clear(self, sems):
        for s in sems:
            self.nc.gpsimd.sem_clear(s)
        self.nc.all_engine_barrier()


def modulation(k):
    nc = k.nc
    with ExitStack() as c:
        w = [k.sb(c, f"wm{b}", [P, KT, 512]) for b in range(2)]
        cc = k.sb(c, "cc", [P, 2, KT])
        t0 = k.sb(c, "t0", [P, 2, KT])
        sc = k.sb(c, "sc", [P, KT, 2])
        bm = k.sb(c, "bm", [P, DEPTH, 24])
        hl = k.sb(c, "hl", [P, 2, 2, 2])
        hd = k.sb(c, "hd", [P, 2, 2, 6])
        lb = k.sb(c, "lb", [P, 2, 2, 2])
        ps = k.bank
        s = k.sems(c, "w_in0 w_in1 w_free small_in mod_mm mod_out act_step dve_step stores_done sigma_e sc_ready lb_e lb_l turns")
        with nc.Block() as block:
            @block.sync
            def _(sp):
                sp.sem_inc(s["w_free"], 2)
                sp.dma_start(cc[:, 0], k.x["c"].rearrange("a (k p) -> p (a k)", p=P)).then_inc(s["small_in"], 16)
                sp.dma_start(cc[:, 1], k.x["c_ctx"].rearrange("(k p) -> p k", p=P)).then_inc(s["small_in"], 16)
                for l in range(DEPTH):
                    sp.dma_start(bm[:, l], k.x["b_mod"][l].rearrange("(m p) -> p m", p=P)).then_inc(s["small_in"], 16)
                for r in range(2):
                    for l in range(DEPTH):
                        sp.dma_start(hl[:, :, r, l], k.x["hg_lower"][r, l].rearrange("(t p) -> p t", p=P)) \
                            .then_inc(s["small_in"], 16)
                for l in range(DEPTH):
                    wl = k.x["w_mod"][l].rearrange("(k p) n -> p k n", p=P)
                    with sp.Fori(0, 3) as i:
                        for b in range(2):
                            hold(sp, s["w_free"], i * 2 + (l * 6 + b + 1), s["turns"])
                            sp.dma_start(w[b][:], wl[:, :, bass.ds((i * 2 + b) * 512, 512)]).then_inc(s[f"w_in{b}"], 16)
                sp.wait_ge(s["mod_out"], 12)
                for l in range(DEPTH):
                    for a in range(2):
                        sp.dma_start(k.modrow[l, a].rearrange("(m p) -> p m", p=P), k.mod[:, l, :, a]) \
                            .then_inc(s["stores_done"], 16)
                sp.wait_ge(s["lb_l"], 1)
                for r in range(2):
                    for d in range(2):
                        sp.dma_start(k.rows[1, r, d * 256:(d + 1) * 256].rearrange("(t p) -> p t", p=P),
                                     lb[:, r, d]).then_inc(s["stores_done"], 16)
                sp.wait_ge(s["stores_done"], 16 * (2 * DEPTH + 4))

            @block.scalar
            def _(act):
                act.preload_act_table_set(TABLES)
                act.wait_ge(s["small_in"], 16 * 8)
                nc.scalar.activation(t0[:], cc[:], ACT.Exp, scale=-1.0).then_inc(s["sigma_e"], 1)
                act.wait_ge(s["lb_e"], 1)
                nc.scalar.activation(hd[:, :, :, 2], hd[:, :, :, 1], ACT.Exp).then_inc(s["act_step"], 1)
                act.wait_ge(s["act_step"], 1)
                nc.scalar.activation(hd[:, :, :, 3], hd[:, :, :, 2], ACT.Ln, bias=1.0).then_inc(s["lb_e"], 1)

            @block.vector
            def _(dve):
                st = Steps(dve, s["dve_step"])
                dve.wait_ge(s["small_in"], 16 * 8)
                st.then(nc.vector.tensor_tensor(hd[:, :, :, 0], hl[:, :, :, 1], hl[:, :, :, 0], ALU.subtract))
                nc.vector.scalar_tensor_tensor(hd[:, :, :, 1], hd[:, :, :, 0], -1.0, hd[:, :, :, 0], ALU.mult, ALU.min) \
                    .then_inc(s["lb_e"], 1)
                dve.wait_ge(s["sigma_e"], 1)
                st.then(nc.vector.tensor_scalar(t0[:], t0[:], 1.0, None, ALU.add))
                st.then(nc.vector.reciprocal(t0[:], t0[:]))
                nc.vector.tensor_tensor(sc[:].rearrange("p k a -> p a k"), cc[:], t0[:], ALU.mult).then_inc(s["sc_ready"], 1)
                dve.wait_ge(s["lb_e"], 2)
                for d in range(2):
                    nc.vector.scalar_tensor_tensor(lb[:, 1, d], hd[:, :, d, 0], 0.0, hd[:, :, d, 3], ALU.min, ALU.subtract)
                st.then(nc.vector.tensor_scalar(hd[:, :, :, 4], hd[:, :, :, 0], -1.0, 0.0, ALU.mult, ALU.min))
                for d in range(2):
                    ins = nc.vector.tensor_tensor(lb[:, 0, d], hd[:, :, d, 4], hd[:, :, d, 3], ALU.subtract)
                ins.then_inc(s["lb_l"], 1)
                for l in range(DEPTH):
                    with dve.Fori(0, 3) as i:
                        for b in range(2):
                            n = l * 6 + b
                            dve.wait_ge(s["mod_mm"], i * 2 + (n + 1))
                            m0 = (i * 2 + b) * 4
                            o = k.mod[:, l, bass.ds(m0, 4), :]
                            nc.vector.tensor_tensor(o, ps[b][:, 0:8].rearrange("p (m a) -> p m a", a=2),
                                                    bm[:, l, bass.ds(m0, 4)].unsqueeze(2).to_broadcast([P, 4, 2]),
                                                    ALU.add).then_inc(s["mod_out"], 1)

            @block.tensor
            def _(pe):
                pe.wait_ge(s["sc_ready"], 1)
                for l in range(DEPTH):
                    with pe.Fori(0, 3) as i:
                        for b in range(2):
                            pe.wait_ge(s[f"w_in{b}"], i * 16 + (l * 3 + 1) * 16)
                            for m in range(4):
                                for q in range(KT):
                                    ins = nc.tensor.matmul(ps[b][:, 2 * m:2 * m + 2], w[b][:, q, m * P:(m + 1) * P],
                                                           sc[:, q], start=(q == 0), stop=(q == KT - 1))
                            ins.then_inc(s["mod_mm"], 1)
                            pe.wait_ge(s["mod_mm"], i * 2 + (l * 6 + b + 1))
                            pe.wait_ge(s["mod_out"], i * 2 + (l * 6 + b + 1))
                            pe.sem_inc(s["w_free"], 1)
        k.clear(s.values())


def hold(sp, sem, value, turns):
    sp.wait_ge(sem, value)
    sp.sem_inc(turns, 1)


def layer_input(k, l):
    if l == 0:
        return (k.x["ctx"][0].rearrange("(t p) n -> t p n", p=P), k.x["x"][0].rearrange("(t p) n -> t p n", p=P))
    return k.stream[0:CT], k.stream[CT:NT]


def projection(k, l):
    nc = k.nc
    RING = 5
    plain = {0: [(0, 256, 1.0), (256, 256, DH ** -0.5)], 1: [(512, 256, 1.0)], 2: [(1024, 16, 1.0)],
             3: [(OFF["da_q"], 512, 1.0)], 4: [(OFF["da_v"], 256, 1.0)], 5: [(OFF["ss_xbc"], 512, 1.0)],
             6: [(2832, 264, 1.0)], 7: [], 8: [(OFF["hg_f"], 512, 1.0)], 9: [(OFF["hg_i"], 256, 1.0)]}
    gated = {1: (768, 256, "sigmoid"), 2: (1040, 256, "silu"), 4: (OFF["da_z"], 256, "silu"),
             7: (OFF["ss_z"], 512, "silu"), 9: (OFF["hg_z"], 256, "silu")}
    order = sorted(gated)
    with ExitStack() as c:
        W = k.sb(c, "W", [P, KT, DIN])
        xt = [k.sb(c, f"xt{b}", [P, D]) for b in range(2)]
        hT = [k.sb(c, f"hT{b}", [P, KT, P]) for b in range(2)]
        u = k.sb(c, "ut", [P, DIN])
        e = [k.sb(c, f"e{b}", [P, 512]) for b in range(2)]
        h = [k.sb(c, f"h{b}", [P, 512]) for b in range(3)]
        kk = k.sb(c, "kk", [P, 512])
        lbr = k.sb(c, "lbr", [P, 2, 512]) if l else None
        small = [k.sb(c, f"small{b}", [P, 8]) for b in range(2)]
        G = k.sb(c, "G", [P, KT, 2])
        ng = k.sb(c, "ng", [P, KT])
        epsc = k.sb(c, "epsc", [P, 1])
        ps = k.bank
        junk = ps[7]
        s = k.sems(c, "w_in x_free small_in g_ready xn_ready xT_mm hT_ready block_mm act_step dve_step "
                      "exp_done e_free copied gated_done lf_neg lf_log lf_key kk_ready lf_neg2 lf_log2 lf_done "
                      + " ".join(f"bank_free{b}" for b in range(RING)) + " " + " ".join(f"st{n}" for n in range(10))
                      + " st_row0 st_row1 st_dt st_kk turns")

        own = list(s.values())
        s.update(k.queue_sems)

        def rounds(eng):
            for kind, first, n in ((1, 0, 1), (0, 1, (NT - CT) // 2)):
                with eng.Fori(0, n) as i:
                    yield i + first, kind, i * 2

        with nc.Block() as block:
            @block.gpsimd
            def _(gp):
                xc_, xl = layer_input(k, l)
                gp.memset(epsc[:], EPS).then_inc(s["g_ready"], 1)
                gp.sem_inc(s["x_free"], 2)
                for r, kind, i in rounds(gp):
                    for b in range(2):
                        gp.wait_ge(s["x_free"], r * 2 + (b + 1))
                        gp.dma_start(xt[b][:], (xc_ if kind else xl)[i + b]).then_inc(s[f"x_in{b}"], 16)

            @block.sync
            def _(sp):
                for n in [f"st{n}" for n in range(10)] + ["st_row0", "st_row1", "st_dt", "st_kk"]:
                    sp.sem_inc(s[n], 16)
                sp.dma_start(ng[:], k.x["norm_g"][l].rearrange("(k p) -> p k", p=P)).then_inc(s["small_in"], 16)
                if l:
                    sp.dma_start(lbr[:].rearrange("p a n -> p (a n)"),
                                 k.rows[l].rearrange("a n -> (a n)").unsqueeze(0).to_broadcast([P, 1024])) \
                        .then_inc(s["small_in"], 16)
                wv = k.x["w_in"][l].rearrange("(k p) n -> p k n", p=P)
                for q in range(KT):
                    sp.dma_start(W[:, q], wv[:, q]).then_inc(s["w_in"], 16)
                for r, kind, i in rounds(sp):
                    for b in range(2):
                        t = r * 2 + b
                        for n, (c0, w) in enumerate(BLOCKS):
                            if plain[n] and n != 8:
                                hold(sp, s["copied"], r * 18 + (b * 9 + sum(bool(plain[m]) for m in range(n + 1))), s["turns"])
                            if n in gated:
                                hold(sp, s["gated_done"], r * 10 + (b * 5 + order.index(n) + 1), s["turns"])
                            if n == 8:
                                hold(sp, s["lf_done"], r * 2 + (b + 1), s["turns"])
                                hold(sp, s["kk_ready"], r * 2 + (b + 1), s["turns"])
                                sp.dma_start(k.u[t, :, OFF["hg_k"]:UW], kk[:]).then_inc(s["st_kk"], 16)
                            if n == 5:
                                continue
                            if n == 6:
                                v = u[:, OFF["ss_xbc"]:OFF["ss_xbc"] + XBC]
                                sp.dma_start(k.xbc[t + 1, 1:P + 1], v).then_inc(s["st6"], 16)
                                sp.dma_start(k.xbc[t, P + 1:P + 2], v[0:1]).then_inc(s["st_row0"], 16)
                                sp.dma_start(k.xbc[t + 2, 0:1], v[P - 1:P]).then_inc(s["st_row1"], 16)
                                sp.dma_start(k.u[t, :, OFF["ss_dt"]:OFF["ss_dt"] + 8],
                                             u[:, OFF["ss_dt"]:OFF["ss_dt"] + 8]).then_inc(s["st_dt"], 16)
                                continue
                            sp.dma_start(k.u[t, :, c0:c0 + w], u[:, c0:c0 + w]).then_inc(s[f"st{n}"], 16)
                for n in [f"st{n}" for n in range(10) if n != 5] + ["st_row0", "st_row1", "st_dt", "st_kk"]:
                    sp.wait_ge(s[n], 16 * (NT + 1))

            @block.tensor
            def _(pe):
                pe.wait_ge(s["w_in"], 16 * KT)
                for b in range(RING):
                    pe.sem_inc(s[f"bank_free{b}"], 1)

                def turn(r, b):
                    pe.wait_ge(s["xn_ready"], r * 2 + (b + 1))
                    if b:
                        pe.wait_ge(s["hT_ready"], r * 2 + 1)
                    for q in range(KT):
                        ins = nc.tensor.transpose(ps[5 + q // 4][:, (q % 4) * P:(q % 4 + 1) * P],
                                                  xt[b][:, q * P:(q + 1) * P], k.ident[:])
                    ins.then_inc(s["xT_mm"], 1)

                def products(r, b, n):
                    c0, w = BLOCKS[n]
                    pe.wait_ge(s[f"bank_free{n % RING}"], r * 4 + (2 * b + n // RING + 1))
                    for q in range(KT):
                        ins = nc.tensor.matmul(ps[n % RING][:, 0:w], hT[b][:, q], W[:, q, c0:c0 + w],
                                               start=(q == 0), stop=(q == KT - 1))
                    ins.then_inc(s["block_mm"], 1)

                for r, kind, i in rounds(pe):
                    turn(r, 0)
                    pe.wait_ge(s["hT_ready"], r * 2 + 1)
                    for n in range(5):
                        products(r, 0, n)
                    turn(r, 1)
                    for n in range(5, 10):
                        products(r, 0, n)
                    pe.wait_ge(s["hT_ready"], r * 2 + 2)
                    for n in range(10):
                        products(r, 1, n)

            @block.scalar
            def _(act):
                act.preload_act_table_set(TABLES)
                st = Steps(act, s["act_step"])
                act.wait_ge(s["g_ready"], 1)
                act.sem_inc(s["e_free"], 2)
                for r, kind, i in rounds(act):
                    for b in range(2):
                        act.wait_ge(s[f"x_in{b}"], r * 16 + 16 * (1 + k.loaded_before))
                        if b == 0:
                            pass
                        sm = small[b]
                        for a in range(2):
                            st.then(nc.scalar.activation(junk[:], xt[b][:, a * 512:(a + 1) * 512], ACT.Square,
                                                         accum_out=sm[:, a:a + 1]))
                        st.then(nc.scalar.activation(sm[:, 2:3], sm[:, 0:1], ACT.Identity, bias=sm[:, 1:2]))
                        st.then(nc.scalar.activation(sm[:, 3:4], sm[:, 2:3], ACT.Ln, scale=1.0 / D, bias=epsc[:]))
                        st.then(nc.scalar.activation(sm[:, 4:5], sm[:, 3:4], ACT.Exp, scale=-0.5))
                        nc.scalar.activation(xt[b][:], xt[b][:], ACT.Copy, scale=sm[:, 4:5]).then_inc(s["xn_ready"], 1)
                    for b in range(2):
                        t = r * 2 + b
                        for n, (c0, w) in enumerate(BLOCKS):
                            act.wait_ge(s["block_mm"], r * 20 + (b * 10 + n + 1))
                            bank = ps[n % RING]
                            act.wait_ge(s["st6" if n == 5 else f"st{n}"], t * 16 + 16)
                            if n in (5, 6):
                                act.wait_ge(s["st_row0"], t * 16 + 16)
                                act.wait_ge(s["st_row1"], t * 16 + 16)
                            if n == 6:
                                act.wait_ge(s["st_dt"], t * 16 + 16)
                            for a, wd, f in plain[n]:
                                ins = nc.scalar.activation(u[:, a:a + wd], bank[:, a - c0:a - c0 + wd], ACT.Copy, scale=f)
                            if plain[n]:
                                ins.then_inc(s["copied"], 1)
                            if n in gated:
                                a, wd, _k = gated[n]
                                g = order.index(n)
                                act.wait_ge(s["e_free"], r * 10 + (b * 5 + g + 1))
                                nc.scalar.activation(e[g % 2 if b == 0 else (g + 1) % 2][:, 0:wd],
                                                     bank[:, a - c0:a - c0 + wd], ACT.Exp, scale=-1.0) \
                                    .then_inc(s["exp_done"], 1)
                            elif n != 8:
                                act.wait_ge(s["copied"], r * 18 + (b * 9 + sum(bool(plain[m]) for m in range(n + 1))))
                                act.sem_inc(s[f"bank_free{n % RING}"], 1)
                            if n == 8:
                                act.wait_ge(s["copied"], r * 18 + (b * 9 + 8))
                                act.sem_inc(s[f"bank_free{n % RING}"], 1)
                                act.wait_ge(s["lf_neg"], r * 2 + (b + 1))
                                st.then(nc.scalar.activation(h[0][:], h[0][:], ACT.Exp))
                                nc.scalar.activation(h[1][:], h[0][:], ACT.Ln, bias=1.0).then_inc(s["lf_log"], 1)
                                act.wait_ge(s["lf_key"], r * 2 + (b + 1))
                                act.wait_ge(s["st_kk"], t * 16 + 16)
                                nc.scalar.activation(kk[:], h[2][:], ACT.Exp).then_inc(s["kk_ready"], 1)
                                if l:
                                    act.wait_ge(s["lf_neg2"], r * 2 + (b + 1))
                                    st.then(nc.scalar.activation(h[0][:], h[0][:], ACT.Exp))
                                    nc.scalar.activation(h[0][:], h[0][:], ACT.Ln, bias=1.0).then_inc(s["lf_log2"], 1)
                    st.clear()

            @block.vector
            def _(dve):
                st = Steps(dve, s["dve_step"])
                dve.wait_ge(s["small_in"], 16 * (1 + bool(l)))
                for a in range(2):
                    st.then(nc.vector.tensor_scalar(G[:, :, a], k.mod[:, l, KT:2 * KT, a], 1.0, None, ALU.add))
                    st.then(nc.vector.tensor_tensor(G[:, :, a], G[:, :, a], ng[:], ALU.mult))
                st.clear()

                def modulate(r, b, kind):
                    dve.wait_ge(s["xT_mm"], r * 2 + (b + 1))
                    dve.sem_inc(s["x_free"], 1)
                    for q in range(KT):
                        ins = nc.vector.tensor_scalar(hT[b][:, q], ps[5 + q // 4][:, (q % 4) * P:(q % 4 + 1) * P],
                                                      G[:, q, kind:kind + 1], k.mod[:, l, q, kind:kind + 1],
                                                      ALU.mult, ALU.add)
                    ins.then_inc(s["hT_ready"], 1)

                for r, kind, i in rounds(dve):
                    modulate(r, 0, kind)
                    for b in range(2):
                        for n in range(10):
                            c0, w = BLOCKS[n]
                            if n == 5 and b == 0:
                                modulate(r, 1, kind)
                            if n in gated:
                                a, wd, how = gated[n]
                                g = order.index(n)
                                dve.wait_ge(s["exp_done"], r * 10 + (b * 5 + g + 1))
                                eb = e[g % 2 if b == 0 else (g + 1) % 2][:, 0:wd]
                                st.then(nc.vector.tensor_scalar(eb, eb, 1.0, None, ALU.add))
                                if how == "sigmoid":
                                    ins = nc.vector.reciprocal(u[:, a:a + wd], eb)
                                else:
                                    st.then(nc.vector.reciprocal(eb, eb))
                                    ins = nc.vector.tensor_tensor(u[:, a:a + wd], bank_of(ps, n)[:, a - c0:a - c0 + wd],
                                                                  eb, ALU.mult)
                                ins.then_inc(s["gated_done"], 1)
                                dve.wait_ge(s["gated_done"], r * 10 + (b * 5 + g + 1))
                                dve.sem_inc(s["e_free"], 1)
                                dve.sem_inc(s[f"bank_free{n % RING}"], 1)
                            if n == 8:
                                z = u[:, OFF["hg_f"]:OFF["hg_f"] + 512]
                                dve.wait_ge(s["copied"], r * 18 + (b * 9 + 8))
                                nc.vector.scalar_tensor_tensor(h[0][:], z, -1.0, z, ALU.mult, ALU.min) \
                                    .then_inc(s["lf_neg"], 1)
                                dve.wait_ge(s["lf_log"], r * 2 + (b + 1))
                                st.then(nc.vector.scalar_tensor_tensor(h[1][:], z, 0.0, h[1][:], ALU.min, ALU.subtract))
                                if l:
                                    st.then(nc.vector.tensor_tensor(h[1][:], h[1][:], lbr[:, 0], ALU.add))
                                nc.vector.tensor_tensor(h[2][:], h[1][:], z, ALU.subtract).then_inc(s["lf_key"], 1)
                                dve.wait_ge(s["lf_key"], r * 2 + (b + 1))
                                if l:
                                    st.then(nc.vector.tensor_tensor(z, h[1][:], lbr[:, 1], ALU.subtract))
                                    nc.vector.scalar_tensor_tensor(h[0][:], z, -1.0, z, ALU.mult, ALU.min) \
                                        .then_inc(s["lf_neg2"], 1)
                                    st.then(nc.vector.tensor_tensor(h[1][:], h[1][:], lbr[:, 1], ALU.max))
                                    dve.wait_ge(s["lf_log2"], r * 2 + (b + 1))
                                    nc.vector.tensor_tensor(z, h[1][:], h[0][:], ALU.add).then_inc(s["lf_done"], 1)
                                else:
                                    nc.vector.tensor_copy(z, h[1][:]).then_inc(s["lf_done"], 1)
                    st.clear()
        k.loaded_before += NT // 2
        k.clear(own)


def bank_of(ps, n):
    return ps[n % 5]


class Banks:

    def __init__(self, k, c, jobs):
        self.k = k
        self.place, self.per = {}, {}
        for bank, names in jobs.items():
            for i, n in enumerate(names.split()):
                self.place[n] = (bank, i)
            self.per[bank] = len(names.split())
        self.full = {b: k.sem(c, f"bank{b}_full") for b in jobs}
        self.free = {b: k.sem(c, f"bank{b}_free") for b in jobs}

    def __getitem__(self, job):
        return self.k.bank[self.place[job][0]]

    def credit(self, eng):
        for b in self.free:
            eng.sem_inc(self.free[b], 1)

    def take(self, pe, job, n):
        b, i = self.place[job]
        pe.wait_ge(self.free[b], n * self.per[b] + (i + 1))

    def done(self, ins, job):
        ins.then_inc(self.full[self.place[job][0]], 1)

    def wait(self, eng, job, n):
        b, i = self.place[job]
        eng.wait_ge(self.full[b], n * self.per[b] + (i + 1))

    def release(self, ins, job):
        ins.then_inc(self.free[self.place[job][0]], 1)

    def sems(self):
        return list(self.full.values()) + list(self.free.values())


def gates(k, l):
    nc = k.nc
    with ExitStack() as c:
        gi = k.sb(c, "gi", [P, NT, 16])
        gd = k.sb(c, "gd", [P, NT, 8])
        gb = k.sb(c, "gb", [P, 2, 2, H])
        dtb = k.sb(c, "dtb", [P, 8])
        al = k.sb(c, "al", [P, 8])
        t0 = k.sb(c, "t0", [P, NT, 16])
        t1 = k.sb(c, "t1", [P, NT, 16])
        t2 = k.sb(c, "t2", [P, NT, 8])
        li = k.sb(c, "li", [P, NT, 8])
        mt = k.sb(c, "mt", [P, NT, 8])
        me = k.sb(c, "me", [P, NT, 8])
        ms = k.sb(c, "ms", [P, NT, 8])
        arg = k.sb(c, "arg", [P, 5, NT, 8])
        GT = k.sb(c, "GT", [P, NT, GW])
        R = k.sb(c, "R", [H, 2, 2, NT, P])
        M = k.sb(c, "M", [H, 2, NT, P])
        NM = k.sb(c, "NM", [H, 2, NT, P])
        ones = k.sb(c, "ones", [P, P])
        tri = k.sb(c, "tri", [P, 4, P])
        pick = k.sb(c, "pick", [P, 2, P])
        ps = k.bank
        s = k.sems(c, "loaded raw_done e_done gate_done row_mm row_copied m_done mt_mm mt_copied end_mm end_copied "
                      "sum_mm arg_ready out_ready stored dve_step act_step gp_ready a_ready")
        col = lambda n: GT[:, :, GC[n]:GC[n] + 8]
        jobs = [(kind, d, q) for kind in range(2) for d in range(2) for q in range((NT + 3) // 4)]
        with nc.Block() as block:
            @block.sync
            def _(sp):
                ld = [(gi[:], k.u[:, :, OFF["ml_i"]:OFF["ml_i"] + 16].rearrange("t p n -> p t n")),
                      (gd[:], k.u[:, :, OFF["ss_dt"]:OFF["ss_dt"] + 8].rearrange("t p n -> p t n")),
                      (gb[:].rearrange("p a b h -> p (a b h)"),
                       k.x["ml_gate_b"][l].rearrange("a b h -> (a b h)").unsqueeze(0).to_broadcast([P, 16])),
                      (dtb[:], k.x["ss_dt_bias"][l].rearrange("a h -> (a h)").unsqueeze(0).to_broadcast([P, 8])),
                      (al[:], k.x["ss_a_log"][l].rearrange("a h -> (a h)").unsqueeze(0).to_broadcast([P, 8])),
                      (tri[:], k.x["c_tri"]), (pick[:], k.x["c_pick"])]
                for o, i in ld:
                    sp.dma_start(o, i).then_inc(s["loaded"], 16)
                sp.wait_ge(s["m_done"], 1)
                for d in range(2):
                    sp.dma_start(k.gr[:, 0, 4 * d:4 * d + 4].rearrange("t h p -> h t p"), NM[:, d]).then_inc(s["stored"], 16)
                    sp.dma_start(k.gr[:, 1, 4 * d:4 * d + 4].rearrange("t h p -> h t p"), R[:, 0, d]).then_inc(s["stored"], 16)
                sp.wait_ge(s["out_ready"], 1)
                sp.dma_start(k.gt.rearrange("t p n -> p t n"), GT[:]).then_inc(s["stored"], 16)
                sp.wait_ge(s["stored"], 16 * 5)

            @block.gpsimd
            def _(gp):
                gp.memset(ones[:], 1.0).then_inc(s["gp_ready"], 1)

            @block.vector
            def _(dve):
                st = Steps(dve, s["dve_step"])
                V = nc.vector
                dve.wait_ge(s["loaded"], 16 * 7)
                for d in range(2):
                    h = slice(4 * d, 4 * d + 4)
                    V.tensor_tensor(li[:, :, h], gi[:, :, h], gb[:, d, 0].unsqueeze(1).to_broadcast([P, NT, H]), ALU.add)
                    V.tensor_tensor(t0[:, :, h], gi[:, :, 8 + 4 * d:12 + 4 * d],
                                    gb[:, d, 1].unsqueeze(1).to_broadcast([P, NT, H]), ALU.add)
                st.then(V.tensor_tensor(t0[:, :, 8:16], gd[:], dtb[:].unsqueeze(1).to_broadcast([P, NT, 8]), ALU.add))
                V.scalar_tensor_tensor(t1[:], t0[:], -1.0, t0[:], ALU.mult, ALU.min).then_inc(s["raw_done"], 1)
                dve.wait_ge(s["e_done"], 1)
                st.then(V.scalar_tensor_tensor(col("lf"), t0[:, :, 0:8], 0.0, t2[:], ALU.min, ALU.subtract))
                st.then(V.tensor_scalar(arg[:, 0], t1[:, :, 8:16], 1.0, None, ALU.add))
                V.scalar_tensor_tensor(arg[:, 1], arg[:, 0], 1.0, t1[:, :, 8:16], ALU.subtract, ALU.subtract)
                st.then(V.reciprocal(arg[:, 2], arg[:, 0]))
                st.then(V.tensor_tensor(arg[:, 1], arg[:, 1], arg[:, 2], ALU.mult))
                dve.wait_ge(s["e_done"], 2)
                st.then(V.tensor_tensor(t2[:], arg[:, 3], arg[:, 1], ALU.subtract))
                st.then(V.scalar_tensor_tensor(col("dt"), t0[:, :, 8:16], 0.0, t2[:], ALU.max, ALU.add))
                V.scalar_tensor_tensor(col("a"), col("dt"), -1.0, al[:].unsqueeze(1).to_broadcast([P, NT, 8]),
                                       ALU.mult, ALU.mult).then_inc(s["gate_done"], 1)
                dve.wait_ge(s["row_copied"], len(jobs))
                f = lambda a: a.rearrange("h t p -> h (t p)")
                V.tensor_tensor_scan(f(M[:, 0]), f(R[:, 1, 0]), f(R[:, 0, 0]), 0.0, ALU.add, ALU.max)
                st.then(V.tensor_tensor_scan(f(M[:, 1, 0:CT])[:, ::-1], f(R[:, 1, 1, 0:CT])[:, ::-1],
                                             f(R[:, 0, 1, 0:CT])[:, ::-1], 0.0, ALU.add, ALU.max))
                st.then(V.tensor_tensor_scan(f(M[:, 1, CT:NT])[:, ::-1], f(R[:, 1, 1, CT:NT])[:, ::-1],
                                             f(R[:, 0, 1, CT:NT])[:, ::-1], M[:, 1, 0, 0:1], ALU.add, ALU.max))
                V.tensor_scalar(NM[:], M[:], -1.0, None, ALU.mult).then_inc(s["m_done"], 1)
                V.memset(ms[:, 0, 0:4], 0.0)
                V.memset(ms[:, 1, 4:8], 0.0)
                dve.wait_ge(s["end_copied"], 1)
                V.tensor_copy(ms[:, 1:NT, 0:4], me[:, 0:NT - 1, 0:4])
                V.tensor_copy(ms[:, 0, 4:8], me[:, 1, 4:8])
                V.tensor_copy(ms[:, NT - 1, 4:8], me[:, 0, 4:8])
                st.then(V.tensor_copy(ms[:, CT:NT - 1, 4:8], me[:, CT + 1:NT, 4:8]))
                dve.wait_ge(s["sum_mm"], 2)
                sums = ps[6][:, 0:6 * NT * H].rearrange("p (x d t h) -> p x d t h", x=3, d=2, h=H)
                for d in range(2):
                    h = slice(4 * d, 4 * d + 4)
                    V.tensor_tensor(arg[:, 0, :, h], sums[:, 0, d], ms[:, :, h], ALU.add)
                    V.tensor_tensor(arg[:, 1, :, h], sums[:, 1, d], li[:, :, h], ALU.add)
                    st.then(V.tensor_tensor(arg[:, 2, :, h], sums[:, 2, d], ms[:, :, h], ALU.add))
                V.tensor_tensor(arg[:, 0], arg[:, 0], mt[:], ALU.subtract)
                V.tensor_tensor(arg[:, 1], arg[:, 1], me[:], ALU.subtract)
                V.tensor_tensor(arg[:, 2], arg[:, 2], me[:], ALU.subtract).then_inc(s["arg_ready"], 1)
                dve.wait_ge(s["a_ready"], 1)
                for hh in range(2):
                    V.tensor_copy(GT[64 * hh:64 * hh + 64, :, GC["as"]:GC["as"] + 4],
                                  arg[64 * hh:64 * hh + 64, 3, :, hh:8:2])
                V.memset(GT[:, :, GC["as"] + 4:GC["as"] + 8], 0.0)
                V.tensor_tensor(col("ws"), col("ws"), col("dt"), ALU.mult).then_inc(s["out_ready"], 1)

            @block.scalar
            def _(act):
                act.preload_act_table_set(TABLES)
                A = nc.scalar.activation
                st = Steps(act, s["act_step"])
                act.wait_ge(s["loaded"], 16 * 7)
                st.then(A(al[:], al[:], ACT.Exp))
                act.wait_ge(s["raw_done"], 1)
                st.then(A(t1[:], t1[:], ACT.Exp))
                A(t2[:], t1[:, :, 0:8], ACT.Ln, bias=1.0).then_inc(s["e_done"], 1)
                A(arg[:, 3], t1[:, :, 8:16], ACT.Ln, bias=1.0).then_inc(s["e_done"], 1)
                for n, (kind, d, q) in enumerate(jobs):
                    act.wait_ge(s["row_mm"], n + 1)
                    w = min(4, NT - 4 * q) * P
                    A(R[:, kind, d, 4 * q:4 * q + w // P].rearrange("h t p -> h (t p)"), ps[n % 4][0:H, 0:w], ACT.Copy) \
                        .then_inc(s["row_copied"], 1)
                act.wait_ge(s["mt_mm"], 1)
                A(mt[:].rearrange("p t n -> p (t n)"), ps[4][:, 0:NT * 8], ACT.Copy).then_inc(s["mt_copied"], 1)
                act.wait_ge(s["end_mm"], 1)
                for d in range(2):
                    ins = A(me[:, :, 4 * d:4 * d + 4],
                            ps[5][:, NT * H * d:NT * H * (d + 1)].rearrange("p (t h) -> p t h", h=H), ACT.Copy)
                ins.then_inc(s["end_copied"], 1)
                act.wait_ge(s["sum_mm"], 2)
                sums = ps[7][:, 0:6 * NT * H].rearrange("p (x d t h) -> p x d t h", x=3, d=2, h=H)
                for d in range(2):
                    for x, n in enumerate(("cum", "ws", "ea")):
                        A(GT[:, :, GC[n] + 4 * d:GC[n] + 4 * d + 4], sums[:, x, d], ACT.Exp)
                A(col("em"), mt[:], ACT.Exp, scale=-1.0)
                act.wait_ge(s["arg_ready"], 1)
                A(col("wint"), arg[:, 0], ACT.Exp)
                A(col("wk"), arg[:, 1], ACT.Exp)
                A(arg[:, 3], arg[:, 2], ACT.Exp).then_inc(s["a_ready"], 1)

            @block.tensor
            def _(pe):
                T = nc.tensor.matmul
                pe.wait_ge(s["gate_done"], 1)
                pe.wait_ge(s["gp_ready"], 1)
                for n, (kind, d, q) in enumerate(jobs):
                    if n >= 4:
                        pe.wait_ge(s["row_copied"], n - 3)
                    src = GT[:, :, GC["lf"]:GC["lf"] + 8] if kind else li[:]
                    for t in range(4 * q, min(4 * q + 4, NT)):
                        ins = T(ps[n % 4][0:H, (t % 4) * P:(t % 4 + 1) * P], src[:, t, 4 * d:4 * d + 4], k.ident[:],
                                start=True, stop=True)
                    ins.then_inc(s["row_mm"], 1)
                for b, n in ((6, "lf"), (7, "a")):
                    for x, m in enumerate(((0, 1), (2, 3), None)):
                        for d in range(2):
                            o = (2 * x + d) * NT * H
                            ins = T(ps[b][:, o:o + NT * H], tri[:, m[d]] if m else ones[:],
                                    GT[:, :, GC[n] + 4 * d:GC[n] + 4 * d + 4], start=True, stop=True)
                    ins.then_inc(s["sum_mm"], 1)
                pe.wait_ge(s["m_done"], 1)
                for t in range(NT):
                    for d in range(2):
                        ins = T(ps[4][:, 8 * t + 4 * d:8 * t + 4 * d + 4], M[:, d, t], k.ident[0:H, 0:H],
                                start=True, stop=True)
                ins.then_inc(s["mt_mm"], 1)
                pe.wait_ge(s["mt_copied"], 1)
                for d in range(2):
                    ins = T(ps[5][:, NT * H * d:NT * H * (d + 1)], pick[:, d], mt[:, :, 4 * d:4 * d + 4],
                            start=True, stop=True)
                ins.then_inc(s["end_mm"], 1)
        k.clear(s.values())


def tile_rounds(eng, backward):
    for first, n, base in ((0, 1, 0), (CT, (NT - CT) // 2, CT)):
        with eng.Fori(0, n) as i:
            for b in range(2):
                number = i * 2 + (first + b)
                yield number, (i * -2 + (base + 2 * n - 1 - b) if backward else number), b


class StateStep:

    JOBS = "hg_sum ml_hg_inc ss_inc"

    def __init__(self, k, c, d, banks, s):
        self.k, self.d, self.bk, self.s = k, d, banks, s
        self.eh = k.sb(c, "eh", [P, 256])
        self.gh = k.sb(c, "gh", [P, 2])
        self.kp = k.sb(c, "kp", [P, 256])
        self.kh = k.sb(c, "kh", [P, 256])
        self.xw = k.sb(c, "xw", [P, 256])

    SEMS = "st_exp st_weighted"

    def pe_sums(self, pe, n, lf, tri, ones):
        bk, T = self.bk, self.k.nc.tensor.matmul
        bk.take(pe, "hg_sum", n)
        b = bk["hg_sum"]
        T(b[:, 0:256], tri[:, 2 + self.d], lf, start=True, stop=True)
        for p in range(2):
            ins = T(b[:, 256 + p:257 + p], lf[:, p * P:(p + 1) * P], ones[:, 0:1], start=True, stop=True)
        bk.done(ins, "hg_sum")

    def act(self, act, n):
        bk, A = self.bk, self.k.nc.scalar.activation
        bk.wait(act, "hg_sum", n)
        b = bk["hg_sum"]
        A(self.eh[:], b[:, 0:256], ACT.Exp)
        ins = A(self.gh[:], b[:, 256:258], ACT.Exp)
        bk.release(ins, "hg_sum")
        act.wait_ge(bk.free[bk.place["hg_sum"][0]], n * bk.per[bk.place["hg_sum"][0]] + (bk.place["hg_sum"][1] + 2))
        act.sem_inc(self.s["st_exp"], 1)

    def dve_weight(self, dve, n, key, kk, xh, gt):
        V = self.k.nc.vector
        h4 = lambda a: a.rearrange("p (h w) -> p h w", h=H)
        g = lambda name: gt[:, GC[name] + 4 * self.d:GC[name] + 4 * self.d + 4].unsqueeze(2).to_broadcast([P, H, DH])
        V.tensor_tensor(h4(self.kp[:]), h4(key), g("wk"), ALU.mult)
        V.tensor_tensor(h4(self.xw[:]), h4(xh), g("ws"), ALU.mult)
        dve.wait_ge(self.s["st_exp"], n + 1)
        V.tensor_tensor(self.kh[:], kk, self.eh[:], ALU.mult).then_inc(self.s["st_weighted"], 1)

    def pe_increments(self, pe, n, vaug, hv, B):
        bk, T = self.bk, self.k.nc.tensor.matmul
        pe.wait_ge(self.s["st_weighted"], n + 1)
        bk.take(pe, "ml_hg_inc", n)
        b = bk["ml_hg_inc"]
        for h in range(H):
            o = slice(64 * (h % 2), 64 * (h % 2) + 64)
            T(b[o, (h // 2) * 65:(h // 2) * 65 + 65], self.kp[:, h * DH:(h + 1) * DH], vaug[:, h], start=True, stop=True)
            ins = T(b[o, 130 + (h // 2) * 64:194 + (h // 2) * 64], self.kh[:, h * DH:(h + 1) * DH],
                    hv[:, h * DH:(h + 1) * DH], start=True, stop=True)
        bk.done(ins, "ml_hg_inc")
        bk.take(pe, "ss_inc", n)
        for g in range(2):
            ins = T(bk["ss_inc"][:, g * P:(g + 1) * P], B[:, g * P:(g + 1) * P], self.xw[:, g * P:(g + 1) * P],
                    start=True, stop=True)
        bk.done(ins, "ss_inc")

    def dve_update(self, dve, n, S, new, gt):
        V, bk, d = self.k.nc.vector, self.bk, self.d
        bk.wait(dve, "ml_hg_inc", n)
        b = bk["ml_hg_inc"]
        for p in range(2):
            sl = slice(p * 65, p * 65 + 65)
            a = GC["as"] + 2 * d + p
            V.scalar_tensor_tensor(new[:, sl], S[:, sl], gt[:, a:a + 1], b[:, sl], ALU.mult, ALU.add)
            sl = slice(ST_HG + p * 64, ST_HG + p * 64 + 64)
            ins = V.scalar_tensor_tensor(new[:, sl], S[:, sl], self.gh[:, p:p + 1], b[:, sl], ALU.mult, ALU.add)
        bk.release(ins, "ml_hg_inc")
        bk.wait(dve, "ss_inc", n)
        for h in range(H):
            sl = slice(ST_SS + h * 64, ST_SS + h * 64 + 64)
            a = GC["ea"] + 4 * d + h
            ins = V.scalar_tensor_tensor(new[:, sl], S[:, sl], gt[:, a:a + 1], bk["ss_inc"][:, h * 64:h * 64 + 64],
                                         ALU.mult, ALU.add)
        bk.release(ins, "ss_inc")
        b, i = bk.place["ss_inc"]
        dve.wait_ge(bk.free[b], n * bk.per[b] + (i + 2))
        b, i = bk.place["ml_hg_inc"]
        dve.wait_ge(bk.free[b], n * bk.per[b] + (i + 2))


def states(k, l):
    nc = k.nc
    NLOAD = 9
    with ExitStack() as c:
        key = [k.sb(c, f"key{b}", [P, 256]) for b in range(2)]
        va = [k.sb(c, f"va{b}", [P, H, 65]) for b in range(2)]
        lf = [k.sb(c, f"lf{b}", [P, 256]) for b in range(2)]
        kk = [k.sb(c, f"kk{b}", [P, 256]) for b in range(2)]
        hv = [k.sb(c, f"hv{b}", [P, 256]) for b in range(2)]
        gt = [k.sb(c, f"gt{b}", [P, GW]) for b in range(2)]
        x3 = [k.sb(c, f"x3{b}", [P, 3, XBC]) for b in range(2)]
        xc = k.sb(c, "xc", [P, XBC])
        xe = k.sb(c, "xe", [P, XBC])
        cw = k.sb(c, "cw", [P, 3, XBC])
        cb = k.sb(c, "cb", [P, XBC])
        S = [k.sb(c, f"S{b}", [P, STW]) for b in range(2)]
        ones = k.sb(c, "ones", [P, 1])
        zero = k.sb(c, "zero", [1, XBC])
        tri = k.sb(c, "tri", [P, 4, P])
        s = k.sems(c, "consts_in memsets zero_rows in0 in1 tile_done dve_step conv_gp conv_sum conv_exp conv_done "
                      "st_exp st_weighted st_stored0 st_stored1 xc_stored turns new_state act_step pe_step")
        bk = Banks(k, c, {0: "hg_sum", 1: "ml_hg_inc", 2: "ss_inc"})
        ss = StateStep(k, c, 1, bk, s)
        ENG = 4
        with nc.Block() as block:
            @block.sync
            def _(sp):
                sp.sem_inc(s["tile_done"], 2 * ENG)
                sp.dma_start(cw[:].rearrange("p a n -> p (a n)"),
                             k.x["ss_conv_w"][l].rearrange("a n -> (a n)").unsqueeze(0).to_broadcast([P, 3 * XBC])) \
                    .then_inc(s["consts_in"], 16)
                sp.dma_start(cb[:], k.x["ss_conv_b"][l].unsqueeze(0).to_broadcast([P, XBC])).then_inc(s["consts_in"], 16)
                sp.dma_start(tri[:], k.x["c_tri"]).then_inc(s["consts_in"], 16)
                sp.wait_ge(s["memsets"], 1)
                for slot, row in () if "xbc" in k.preset else ((1, 0), (CT, P + 1), (CT + 1, 0), (NT, P + 1)):
                    sp.dma_start(k.xbc[slot, row:row + 1], zero[:]).then_inc(s["zero_rows"], 16)
                sp.wait_ge(s["zero_rows"], 64) if "xbc" not in k.preset else None
                for n, t, b in tile_rounds(sp, True):
                    hold(sp, s["tile_done"], n * ENG + ENG, s["turns"])
                    u = k.u[t]
                    ld = [(key[b][:], u[:, 256:512]),
                          (va[b][:, :, 0:64], u[:, 512:768].rearrange("p (h w) -> p h w", h=H)),
                          (lf[b][:], u[:, OFF["hg_f"] + 256:OFF["hg_f"] + 512]),
                          (kk[b][:], u[:, OFF["hg_k"] + 256:OFF["hg_k"] + 512]),
                          (hv[b][:], u[:, OFF["hg_i"]:OFF["hg_i"] + 256]),
                          (gt[b][:], k.gt[t])] + [(x3[b][:, a], k.xbc[t + 1, a:a + P]) for a in range(3)]
                    assert len(ld) == NLOAD
                    for o, i in ld:
                        sp.dma_start(o, i).then_inc(s[f"in{b}"], 16)

            @block.gpsimd
            def _(gp):
                G = nc.gpsimd
                gp.memset(zero[:], 0.0)
                gp.memset(ones[:], 1.0)
                for b in range(2):
                    gp.memset(va[b][:, :, 64:65], 1.0)
                gp.memset(S[0][:], 0.0).then_inc(s["memsets"], 1)
                gp.wait_ge(s["consts_in"], 48)
                for n, t, b in tile_rounds(gp, True):
                    gp.wait_ge(s["tile_done"], n * ENG + 2 * ENG)
                    gp.wait_ge(s[f"in{b}"], per_buffer(n, b, NLOAD))
                    G.tensor_tensor(x3[b][:, 2], x3[b][:, 2], cw[:, 2], ALU.mult).then_inc(s["conv_gp"], 1)
                    gp.wait_ge(s["conv_gp"], n * 2 + 1)
                    G.tensor_tensor(x3[b][:, 2], x3[b][:, 2], cb[:], ALU.add).then_inc(s["conv_gp"], 1)
                    gp.wait_ge(s["conv_gp"], n * 2 + 2)
                    gp.sem_inc(s["tile_done"], 1)

            @block.vector
            def _(dve):
                V = nc.vector
                st = Steps(dve, s["dve_step"])
                dve.wait_ge(s["consts_in"], 48)
                dve.wait_ge(s["memsets"], 1)
                for n, t, b in tile_rounds(dve, True):
                    dve.wait_ge(s["tile_done"], n * ENG + 2 * ENG)
                    dve.wait_ge(s[f"in{b}"], per_buffer(n, b, NLOAD))
                    V.tensor_tensor(x3[b][:, 0], x3[b][:, 0], cw[:, 0], ALU.mult)
                    st.then(V.tensor_tensor(x3[b][:, 1], x3[b][:, 1], cw[:, 1], ALU.mult))
                    st.then(V.tensor_tensor(x3[b][:, 0], x3[b][:, 0], x3[b][:, 1], ALU.add))
                    dve.wait_ge(s["conv_gp"], n * 2 + 2)
                    V.tensor_tensor(x3[b][:, 0], x3[b][:, 0], x3[b][:, 2], ALU.add).then_inc(s["conv_sum"], 1)
                    dve.wait_ge(s["conv_exp"], n + 1)
                    st.then(V.tensor_scalar(xe[:], xe[:], 1.0, None, ALU.add))
                    st.then(V.reciprocal(xe[:], xe[:]))
                    dve.wait_ge(s["xc_stored"], n * 16 + 16)
                    V.tensor_tensor(xc[:], x3[b][:, 0], xe[:], ALU.mult).then_inc(s["conv_done"], 1)
                    dve.wait_ge(s["conv_done"], n + 1)
                    ss.dve_weight(dve, n, key[b][:], kk[b][:], xc[:, 0:256], gt[b])
                    dve.wait_ge(s[f"st_stored{1 - b}"], (n - b) * 8 + (16 + 16 * b) if b == 0 else (n - b) * 8 + 32)
                    ss.dve_update(dve, n, S[b], S[1 - b], gt[b])
                    dve.sem_inc(s["new_state"], 1)
                    st.clear()
                    dve.sem_inc(s["tile_done"], 1)

            @block.scalar
            def _(act):
                act.preload_act_table_set(TABLES)
                A = nc.scalar.activation
                act.sem_inc(s["xc_stored"], 16)
                act.sem_inc(s["st_stored1"], 16)
                act.sem_inc(s["st_stored0"], 16)
                act.wait_ge(s["memsets"], 1)
                for n, t, b in tile_rounds(act, True):
                    act.wait_ge(s["tile_done"], n * ENG + 2 * ENG)
                    act.dma_start(k.st[t], S[b][:]).then_inc(s[f"st_stored{b}"], 16)
                    act.wait_ge(s["conv_sum"], n + 1)
                    A(xe[:], x3[b][:, 0], ACT.Exp, scale=-1.0).then_inc(s["conv_exp"], 1)
                    ss.act(act, n)
                    act.wait_ge(s["conv_done"], n + 1)
                    act.dma_start(k.xc[t], xc[:]).then_inc(s["xc_stored"], 16)
                    act.sem_inc(s["tile_done"], 1)
                act.wait_ge(s["xc_stored"], 16 * (NT + 1))
                for b in range(2):
                    act.wait_ge(s[f"st_stored{b}"], 16 * (NT // 2 + 1))

            @block.tensor
            def _(pe):
                bk.credit(pe)
                pe.wait_ge(s["consts_in"], 48)
                pe.wait_ge(s["memsets"], 1)
                for n, t, b in tile_rounds(pe, True):
                    pe.wait_ge(s["tile_done"], n * ENG + 2 * ENG)
                    pe.wait_ge(s[f"in{b}"], per_buffer(n, b, NLOAD))
                    ss.pe_sums(pe, n, lf[b][:], tri, ones)
                    pe.wait_ge(s["conv_done"], n + 1)
                    ss.pe_increments(pe, n, va[b], hv[b], xc[:, 256:512])
                    bk.wait(pe, "ss_inc", n)
                    pe.sem_inc(s["tile_done"], 1)
        k.clear(list(s.values()) + bk.sems())


def per_buffer(n, b, loads):
    return (n - b) * (8 * loads) + 16 * loads


def mixing(k, l):
    nc = k.nc
    NLOAD = 9
    ENG = 4
    JOBS = {0: "ml_T ml_S0 ml_own0 ml_own1", 1: "ml_arg0 ml_arg1 ml_past0 ml_past1",
            2: "ss_T ss_CB ss_past ml_hg_inc", 3: "ss_arg0 ss_arg1 ss_own ss_inc hg_out1",
            4: "hg_qT hg_kT hg_sum hg_out0", 5: "ml_S1 " + " ".join(f"hg_E{v}" for v in range(LEVELS + 1)),
            6: " ".join(f"hg_A0_{v}" for v in range(LEVELS + 1)), 7: " ".join(f"hg_A1_{v}" for v in range(LEVELS + 1))}
    HO = {n: OFF[n] - OFF["ss_z"] for n in ("ss_z", "hg_q", "hg_f", "hg_i", "hg_z", "hg_k")}
    with ExitStack() as c:
        two = lambda name, shape: [k.sb(c, f"{name}{b}", shape) for b in range(2)]
        qk = two("qk", [P, 512])
        va = two("va", [P, H, 65])
        og = two("og", [P, 2, 256])
        hg = two("hg", [P, UW - OFF["ss_z"]])
        xc = two("xc", [P, XBC])
        gt = two("gt", [P, GW])
        gr = two("gr", [H, 2, 2, P])
        sB = two("sB", [P, STW])
        S = two("S", [P, STW])
        qkT = k.sb(c, "qkT", [P, 4, P])
        bcT = k.sb(c, "bcT", [P, 4, P])
        hqT = k.sb(c, "hqT", [P, 2, P])
        hkT = k.sb(c, "hkT", [P, 2, 2, P])
        ltri = k.sb(c, "ltri", [P, 2, H, P])
        atri = k.sb(c, "atri", [P, 2, H, P])
        Pm = two("Pm", [P, H, P])
        sP = two("sP", [P, H, P])
        L = two("L", [P, H, P])
        xd = two("xd", [P, 256])
        E = two("E", [P, 2, 2, P])
        Xq = two("Xq", [P, 2, 2, P])
        Xk = two("Xk", [P, 2, 2, P])
        Aw = two("Aw", [P, 2, 2, P])
        num = k.sb(c, "num", [P, 2, 2, 2, 65])
        den = k.sb(c, "den", [P, 2, 2, 2])
        hm = k.sb(c, "hm", [P, 256])
        ysum = k.sb(c, "ysum", [P, 2, 256])
        yss = k.sb(c, "yss", [P, 256])
        yhg = k.sb(c, "yhg", [P, 256])
        dx = k.sb(c, "dx", [P, 256])
        sq = k.sb(c, "sq", [P, 3, 256])
        mean = k.sb(c, "mean", [P, H])
        ssq = k.sb(c, "ssq", [P, 10])
        rstd = k.sb(c, "rstd", [P, 10])
        yo = k.sb(c, "yo", [P, 3, 256])
        gn = k.sb(c, "gn", [P, 3, 256])
        dsk = k.sb(c, "dsk", [P, H])
        eps = k.sb(c, "eps", [P, 1])
        ones = k.sb(c, "ones", [P, 1])
        tri = k.sb(c, "tri", [P, 4, P])
        mats = k.sb(c, "mats", [P, 2 * LEVELS, P])
        masks = k.sb(c, "masks", [P, 2 * (LEVELS + 1), P])
        neg = k.sb(c, "neg", [P, 2, P])
        negb = k.sb(c, "negb", [P, 2, H, P], BF16)
        idb = k.sb(c, "idb", [P, P], BF16)
        sel = k.sb(c, "sel", [H, H, P])
        s = k.sems(c, "consts_in memsets in0 in1 tile_done dve_step act_step gp_step turns st_exp st_weighted "
                      "ml_T_copied ss_T_copied hg_T_copied masked ml_P ss_L ml_sP ss_sc turns_dve E_ready Xq_ready Xk_ready "
                      "A_ready ssq_ready rstd_ready y_ready y_stored new_state pe_done xd_ready small_ready")
        bk = Banks(k, c, JOBS)
        ss = StateStep(k, c, 0, bk, s)
        consts = [(tri[:], k.x["c_tri"]), (mats[:], k.x["c_mats"]), (masks[:], k.x["c_masks"]), (neg[:], k.x["c_neg"]),
                  (sel[:], k.x["c_sel"][0:H, 0:H]),
                  (gn[:, 0], k.x["ml_norm_g"][l].unsqueeze(0).to_broadcast([P, 256])),
                  (gn[:, 1], k.x["ss_norm_g"][l].unsqueeze(0).to_broadcast([P, 256])),
                  (gn[:, 2], k.x["hg_norm_g"][l].unsqueeze(0).to_broadcast([P, 256])),
                  (dsk[:], k.x["ss_d"][l].unsqueeze(0).to_broadcast([P, H]))]
        h4 = lambda a: a.rearrange("p (h w) -> p h w", h=H)
        gcol = lambda g, name, d: g[:, GC[name] + 4 * d:GC[name] + 4 * d + 4]

        with nc.Block() as block:
            @block.sync
            def _(sp):
                sp.sem_inc(s["tile_done"], 2 * ENG)
                for o, i in consts:
                    sp.dma_start(o, i).then_inc(s["consts_in"], 16)
                sp.wait_ge(s["memsets"], 1)
                for n, t, b in tile_rounds(sp, False):
                    hold(sp, s["tile_done"], n * ENG + ENG, s["turns"])
                    u = k.u[t]
                    ld = [(qk[b][:], u[:, 0:512]),
                          (va[b][:, :, 0:64], u[:, 512:768].rearrange("p (h w) -> p h w", h=H)),
                          (og[b][:, 0], u[:, 768:1024]), (og[b][:, 1], u[:, 1040:1296]),
                          (hg[b][:], u[:, OFF["ss_z"]:UW]), (xc[b][:], k.xc[t]), (gt[b][:], k.gt[t]),
                          (gr[b][:], k.gr[t].rearrange("a (d h) p -> h a d p", h=H)), (sB[b][:], k.st[t])]
                    assert len(ld) == NLOAD
                    for o, i in ld:
                        sp.dma_start(o, i).then_inc(s[f"in{b}"], 16)

            @block.gpsimd
            def _(gp):
                G = nc.gpsimd
                gp.memset(ones[:], 1.0)
                gp.memset(eps[:], EPS)
                for b in range(2):
                    gp.memset(va[b][:, :, 64:65], 1.0)
                    gp.memset(Aw[b][:], 0.0)
                gp.memset(S[0][:], 0.0).then_inc(s["memsets"], 1)
                gp.wait_ge(s["consts_in"], 16 * len(consts))
                st = Steps(gp, s["gp_step"])
                for n, t, b in tile_rounds(gp, False):
                    gp.wait_ge(s["tile_done"], n * ENG + 2 * ENG)
                    gp.wait_ge(s[f"in{b}"], per_buffer(n, b, NLOAD))
                    for d in range(2):
                        for o, name in ((ltri, "lf"), (atri, "a")):
                            G.tensor_tensor(o[:, d], tri[:, 2 + d].unsqueeze(1).to_broadcast([P, H, P]),
                                            gcol(gt[b], name, d).unsqueeze(2).to_broadcast([P, H, P]), ALU.mult) \
                                .then_inc(s["masked"], 1)
                    gp.wait_ge(s["hg_T_copied"], n * 2 + 2)
                    for v in range(LEVELS):
                        gp.wait_ge(s["E_ready"], n * (LEVELS + 1) + (v + 1))
                        if v >= 2:
                            bk.wait(gp, f"hg_A1_{v - 2}", n)
                        G.tensor_tensor(Xk[v % 2][:], E[v % 2][:], hkT[:], ALU.mult).then_inc(s["Xk_ready"], 1)
                    gp.wait_ge(s["Xk_ready"], n * LEVELS + LEVELS)
                    gp.sem_inc(s["tile_done"], 1)

            @block.scalar
            def _(act):
                act.preload_act_table_set(TABLES)
                A = nc.scalar.activation
                act.sem_inc(s["y_stored"], 16)
                act.wait_ge(s["memsets"], 1)
                st = Steps(act, s["act_step"])
                f2 = lambda a: a.rearrange("p a n -> p (a n)")
                f3 = lambda a: a.rearrange("p a b n -> p (a b n)")
                for n, t, b in tile_rounds(act, False):
                    act.wait_ge(s["tile_done"], n * ENG + 2 * ENG)

                    def drain(job, out, sem, func=ACT.Copy, w=512):
                        bk.wait(act, job, n)
                        st.mark(A(out, bk[job][:, 0:w], func))
                        st.wait()
                        act.sem_inc(bk.free[bk.place[job][0]], 1)
                        act.sem_inc(s[sem], 1)

                    drain("ml_T", f2(qkT[:]), "ml_T_copied")
                    drain("ss_T", f2(bcT[:]), "ss_T_copied")
                    drain("hg_qT", f2(hqT[:]), "hg_T_copied", w=256)
                    for d in range(2):
                        drain(f"ml_arg{d}", f2(Pm[d][:]), "ml_P", ACT.Exp)
                    drain("hg_kT", f3(hkT[:]), "hg_T_copied")
                    for d in range(2):
                        drain(f"ss_arg{d}", f2(L[d][:]), "ss_L", ACT.Exp)
                    ss.act(act, n)
                    for v in range(LEVELS + 1):
                        if v >= 2:
                            act.wait_ge(s["Xq_ready"], n * (LEVELS + 1) + (v - 1))
                            act.wait_ge(s["Xk_ready"], n * LEVELS + (v - 1))
                        drain(f"hg_E{v}", f3(E[v % 2][:]), "E_ready", ACT.Exp)
                    act.wait_ge(s["ssq_ready"], n + 1)
                    A(rstd[:, 0:8], ssq[:, 0:8], ACT.Ln, scale=1.0 / 64, bias=eps[:])
                    st.then(A(rstd[:, 8:10], ssq[:, 8:10], ACT.Ln, scale=1.0 / 128, bias=eps[:]))
                    A(rstd[:], rstd[:], ACT.Exp, scale=-0.5).then_inc(s["rstd_ready"], 1)
                    act.wait_ge(s["y_ready"], n + 1)
                    act.dma_start(k.y[t, :, 0:256], yo[:, 0]).then_inc(s["y_stored"], 16)
                    act.dma_start(k.y[t, :, 512:1024].rearrange("p (a n) -> p a n", a=2), yo[:, 1:3]) \
                        .then_inc(s["y_stored"], 16)
                    st.clear()
                    act.sem_inc(s["tile_done"], 1)
                act.wait_ge(s["y_stored"], 32 * NT + 16)

            @block.vector
            def _(dve):
                V = nc.vector
                st = Steps(dve, s["dve_step"])
                dve.wait_ge(s["consts_in"], 16 * len(consts))
                dve.wait_ge(s["memsets"], 1)
                V.tensor_copy(idb[:], k.ident[:])
                V.tensor_copy(negb[:], neg[:].unsqueeze(2).to_broadcast([P, 2, H, P])).then_inc(s["small_ready"], 1)
                for n, t, b in tile_rounds(dve, False):
                    g, hb = gt[b], hg[b]
                    hc = lambda name, w=256: hb[:, HO[name]:HO[name] + w]
                    dve.wait_ge(s["tile_done"], n * ENG + 2 * ENG)
                    dve.wait_ge(s[f"in{b}"], per_buffer(n, b, NLOAD))
                    for d in range(2):
                        ins = V.tensor_tensor(h4(xd[d][:]), h4(xc[b][:, 0:256]),
                                              gcol(g, "dt", d).unsqueeze(2).to_broadcast([P, H, DH]), ALU.mult)
                    ins.then_inc(s["xd_ready"], 1)
                    par = lambda a, x: a.rearrange("p (a x) i -> p x a i", x=2)[:, x]
                    for x in range(2):
                        bk.wait(dve, f"ml_S{x}", n)
                    for d in range(2):
                        dve.wait_ge(s["ml_P"], n * 2 + (d + 1))
                        for x in range(2):
                            ins = V.tensor_tensor(par(sP[d][:], x), bk[f"ml_S{x}"][:, 0:256]
                                                  .rearrange("p (a i) -> p a i", a=2), par(Pm[d][:], x), ALU.mult)
                        ins.then_inc(s["ml_sP"], 1)
                    dve.wait_ge(s["ml_sP"], n * 2 + 2)
                    dve.sem_inc(bk.free[0], 1)
                    dve.sem_inc(bk.free[5], 1)
                    bk.wait(dve, "ss_CB", n)
                    for d in range(2):
                        dve.wait_ge(s["ss_L"], n * 2 + (d + 1))
                        L4 = L[d][:].rearrange("p (g r) i -> p g r i", g=2)
                        V.tensor_tensor(L4, bk["ss_CB"][:, 0:256].rearrange("p (g i) -> p g i", g=2).unsqueeze(2)
                                        .to_broadcast([P, 2, 2, P]), L4, ALU.mult).then_inc(s["ss_sc"], 1)
                    dve.wait_ge(s["ss_sc"], n * 2 + 2)
                    dve.sem_inc(bk.free[2], 1)
                    ss.dve_weight(dve, n, qk[b][:, 256:512], hc("hg_k"), xc[b][:, 0:256], g)

                    def keep(v):
                        for x in range(2):
                            bk.wait(dve, f"hg_A{x}_{v}", n)
                            dve.sem_inc(s["turns_dve"], 1)
                            m = masks[:, 2 * v:2 * v + 2].bitcast(mybir.dt.int32).unsqueeze(2).to_broadcast([P, 2, 2, P])
                            st.then(V.copy_predicated(Aw[x][:], m, bk[f"hg_A{x}_{v}"][:]
                                                      .rearrange("p (d a i) -> p d a i", d=2, a=2)))
                            dve.sem_inc(bk.free[6 + x], 1)

                    dve.wait_ge(s["hg_T_copied"], n * 2 + 2)
                    for v in range(LEVELS + 1):
                        dve.wait_ge(s["E_ready"], n * (LEVELS + 1) + (v + 1))
                        if 2 <= v:
                            bk.wait(dve, f"hg_A1_{v - 2}", n)
                        V.tensor_tensor(Xq[v % 2][:], E[v % 2][:], hqT[:].unsqueeze(1).to_broadcast([P, 2, 2, P]),
                                        ALU.mult).then_inc(s["Xq_ready"], 1)
                        if v >= 1:
                            keep(v - 1)
                        if v == 1:
                            for x in range(2):
                                bk.wait(dve, f"ml_past{x}", n)
                                wint = g[:, GC["wint"]:GC["wint"] + 8].rearrange("p (d a x) -> p x d a", d=2, x=2)[:, x]
                                st.then(V.tensor_tensor(num[:, :, x], bk[f"ml_past{x}"][:, 0:260]
                                                        .rearrange("p (d a w) -> p d a w", d=2, a=2),
                                                        wint.unsqueeze(3).to_broadcast([P, 2, 2, 65]), ALU.mult))
                                dve.sem_inc(bk.free[1], 1)
                            for d in range(2):
                                bk.wait(dve, f"ml_own{d}", n)
                                nd = num[:, d].rearrange("p x a w -> p (x a w)")
                                st.then(V.tensor_tensor(nd, bk[f"ml_own{d}"][:, 0:260], nd, ALU.add))
                                dve.sem_inc(bk.free[0], 1)
                            em = g[:, GC["em"]:GC["em"] + 8].rearrange("p (d a x) -> p d x a", d=2, x=2)
                            dn = num[:, :, :, :, 64]
                            st.then(V.scalar_tensor_tensor(den[:].rearrange("p d x a -> p (d x) a"),
                                                           dn.rearrange("p d x a -> p (d x) a"), -1.0,
                                                           dn.rearrange("p d x a -> p (d x) a"), ALU.mult, ALU.max))
                            st.then(V.tensor_tensor(den[:], den[:], em, ALU.max))
                            st.then(V.reciprocal(den[:], den[:]))
                            for d in range(2):
                                st.mark(V.tensor_tensor(num[:, d, :, :, 0:64], num[:, d, :, :, 0:64],
                                                        den[:, d].unsqueeze(3).to_broadcast([P, 2, 2, DH]), ALU.mult))
                            st.wait()
                            st.then(V.tensor_tensor(hm[:].rearrange("p (a x w) -> p x a w", a=2, x=2),
                                                    num[:, 0, :, :, 0:64], num[:, 1, :, :, 0:64], ALU.add))
                            st.then(V.tensor_tensor(hm[:], hm[:], og[b][:, 0], ALU.mult))
                            st.then(V.tensor_reduce(mean[:], h4(hm[:]), AX.X, ALU.add))
                            st.then(V.tensor_scalar(mean[:], mean[:], 1.0 / DH, None, ALU.mult))
                            st.then(V.tensor_tensor(h4(hm[:]), h4(hm[:]), mean[:].unsqueeze(2).to_broadcast([P, H, DH]),
                                                    ALU.subtract))
                            st.then(V.tensor_tensor(sq[:, 0], hm[:], hm[:], ALU.mult))
                            st.then(V.tensor_reduce(ssq[:, 0:4], h4(sq[:, 0]), AX.X, ALU.add))
                        if v == 4:
                            bk.wait(dve, "ss_past", n)
                            for d in range(2):
                                ins = V.tensor_tensor(h4(ysum[:, d]), h4(bk["ss_past"][:, d * 256:(d + 1) * 256]),
                                                      gcol(g, "cum", d).unsqueeze(2).to_broadcast([P, H, DH]), ALU.mult)
                                st.mark(ins)
                            st.then(V.tensor_tensor(h4(dx[:]), h4(xc[b][:, 0:256]),
                                                    dsk[:].unsqueeze(2).to_broadcast([P, H, DH]), ALU.mult))
                            dve.sem_inc(bk.free[2], 1)
                            st.then(V.tensor_tensor(ysum[:, 0], ysum[:, 0], ysum[:, 1], ALU.add))
                            st.then(V.tensor_tensor(dx[:], dx[:], ysum[:, 0], ALU.add))
                            bk.wait(dve, "ss_own", n)
                            st.then(V.tensor_tensor(yss[:], bk["ss_own"][:, 0:256], dx[:], ALU.add))
                            dve.sem_inc(bk.free[3], 1)
                            st.then(V.tensor_tensor(yss[:], yss[:], hc("ss_z"), ALU.mult))
                            st.then(V.tensor_tensor(sq[:, 1], yss[:], yss[:], ALU.mult))
                            st.then(V.tensor_reduce(ssq[:, 8:10], sq[:, 1].rearrange("p (g w) -> p g w", g=2), AX.X, ALU.add))
                    keep(LEVELS)
                    dve.sem_inc(s["A_ready"], 1)
                    ss.dve_update(dve, n, S[b], S[1 - b], g)
                    for x in range(2):
                        bk.wait(dve, f"hg_out{x}", n)
                        st.then(V.tensor_copy(yhg[:].rearrange("p (a x w) -> p x a w", a=2, x=2)[:, x],
                                              bk[f"hg_out{x}"][:, 0:128].rearrange("p (a w) -> p a w", a=2)))
                    dve.sem_inc(bk.free[4], 1)
                    dve.sem_inc(bk.free[3], 1)
                    st.then(V.tensor_tensor(sq[:, 2], yhg[:], yhg[:], ALU.mult))
                    V.tensor_reduce(ssq[:, 4:8], h4(sq[:, 2]), AX.X, ALU.add).then_inc(s["ssq_ready"], 1)
                    dve.wait_ge(s["rstd_ready"], n + 1)
                    for a, (y, G_, r0, z) in enumerate(((hm, H, 0, og[b][:, 1]), (yss, 2, 8, None), (yhg, H, 4, hc("hg_z")))):
                        W_ = 256 // G_
                        gw = lambda x: x.rearrange("p (g w) -> p g w", g=G_)
                        st.mark(V.tensor_tensor(gw(y[:]), gw(y[:]), rstd[:, r0:r0 + G_].unsqueeze(2)
                                                .to_broadcast([P, G_, W_]), ALU.mult))
                    st.wait()
                    for a, (y, z) in ((0, (hm, og[b][:, 1])), (2, (yhg, hc("hg_z")))):
                        st.mark(V.tensor_tensor(y[:], y[:], z, ALU.mult))
                    st.wait()
                    dve.wait_ge(s["y_stored"], n * 32 + 16)
                    for a, y in ((0, hm), (1, yss), (2, yhg)):
                        ins = V.tensor_tensor(yo[:, a], y[:], gn[:, a], ALU.mult)
                    ins.then_inc(s["y_ready"], 1)
                    dve.wait_ge(s["y_ready"], n + 1)
                    dve.sem_inc(s["tile_done"], 1)
                    st.clear()

            @block.tensor
            def _(pe):
                T = nc.tensor.matmul
                bk.credit(pe)
                pe.wait_ge(s["consts_in"], 16 * len(consts))
                pe.wait_ge(s["memsets"], 1)
                pe.wait_ge(s["small_ready"], 1)

                def turn(job, parts, n):
                    bk.take(pe, job, n)
                    for i, a in enumerate(parts):
                        ins = nc.tensor.transpose(bk[job][:, i * P:(i + 1) * P], a, k.ident[:])
                    bk.done(ins, job)

                def arg(job, d, m, rows, n):
                    bk.take(pe, job, n)
                    b_ = bk[job]
                    T(b_[:], idb[:], negb[:, d].rearrange("p h i -> p (h i)"), start=True, stop=False,
                      skip_group_check=True)
                    for h in range(H):
                        o = b_[:, h * P:(h + 1) * P]
                        if rows is not None:
                            T(o, sel[:, h], rows[:, 0, d], start=False, stop=False, skip_group_check=True)
                            T(o, rows[:, 1, d], sel[:, h], start=False, stop=False, skip_group_check=True)
                        ins = T(o, m[:, d, h], tri[:, d], start=False, stop=True, skip_group_check=True)
                    bk.done(ins, job)

                hh = lambda h: slice(64 * (h % 2), 64 * (h % 2) + 64)
                for n, t, b in tile_rounds(pe, False):
                    hb = hg[b]
                    hc = lambda name, o=0, w=256: hb[:, HO[name] + o:HO[name] + o + w]
                    lfs = hc("hg_f", 0, 512)
                    pe.wait_ge(s["tile_done"], n * ENG + 2 * ENG)
                    pe.wait_ge(s[f"in{b}"], per_buffer(n, b, NLOAD))
                    turn("ml_T", [qk[b][:, i * P:(i + 1) * P] for i in range(4)], n)
                    turn("ss_T", [xc[b][:, 256 + i * P:256 + (i + 1) * P] for i in range(4)], n)
                    turn("hg_qT", [hc("hg_q", i * P, P) for i in range(2)], n)
                    pe.wait_ge(s["ml_T_copied"], n + 1)
                    for x in range(2):
                        bk.take(pe, f"ml_S{x}", n)
                        for p in range(2):
                            ins = T(bk[f"ml_S{x}"][:, p * P:(p + 1) * P], qkT[hh(x), 2 + p], qkT[hh(x), p],
                                    start=True, stop=True)
                        bk.done(ins, f"ml_S{x}")
                    turn("hg_kT", [hc("hg_k", i * P, P) for i in range(4)], n)
                    for d in range(2):
                        pe.wait_ge(s["masked"], n * 4 + (2 * d + 1))
                        arg(f"ml_arg{d}", d, ltri, gr[b], n)
                    pe.wait_ge(s["ss_T_copied"], n + 1)
                    bk.take(pe, "ss_CB", n)
                    for g in range(2):
                        ins = T(bk["ss_CB"][:, g * P:(g + 1) * P], bcT[:, g], bcT[:, 2 + g], start=True, stop=True)
                    bk.done(ins, "ss_CB")
                    for d in range(2):
                        pe.wait_ge(s["masked"], n * 4 + (2 * d + 2))
                        arg(f"ss_arg{d}", d, atri, None, n)
                    ss.pe_sums(pe, n, hc("hg_f"), tri, ones)

                    def level(v):
                        bk.take(pe, f"hg_E{v}", n)
                        for d in range(2):
                            m = mats[:, 2 * v + d] if v < LEVELS else tri[:, d]
                            for p in range(2):
                                i = 2 * d + p
                                ins = T(bk[f"hg_E{v}"][:, i * P:(i + 1) * P], lfs[:, i * P:(i + 1) * P], m,
                                        start=True, stop=True)
                        bk.done(ins, f"hg_E{v}")

                    def weights(v):
                        if v < LEVELS:
                            pe.wait_ge(s["Xq_ready"], n * (LEVELS + 1) + (v + 1))
                            pe.wait_ge(s["Xk_ready"], n * LEVELS + (v + 1))
                        for x in range(2):
                            bk.take(pe, f"hg_A{x}_{v}", n)
                            for d in range(2):
                                for p in range(2):
                                    kx = Xk[v % 2][hh(x), d, p] if v < LEVELS else hkT[hh(x), d, p]
                                    qx = Xq[v % 2][hh(x), d, p] if v < LEVELS else hqT[hh(x), p]
                                    ins = T(bk[f"hg_A{x}_{v}"][:, (2 * d + p) * P:(2 * d + p + 1) * P], kx, qx,
                                            start=True, stop=True)
                            bk.done(ins, f"hg_A{x}_{v}")

                    level(0)
                    level(1)
                    for v in range(LEVELS):
                        weights(v)
                        if v + 2 <= LEVELS:
                            level(v + 2)
                        if v == 0:
                            for x in range(2):
                                bk.take(pe, f"ml_past{x}", n)
                                for d in range(2):
                                    St = S[b] if d == 0 else sB[b]
                                    for p in range(2):
                                        o = (2 * d + p) * 65
                                        ins = T(bk[f"ml_past{x}"][:, o:o + 65], qkT[hh(x), p],
                                                St[hh(x), p * 65:p * 65 + 65], start=True, stop=True)
                                bk.done(ins, f"ml_past{x}")
                            for d in range(2):
                                pe.wait_ge(s["ml_sP"], n * 2 + (d + 1))
                                bk.take(pe, f"ml_own{d}", n)
                                for h in range(H):
                                    o = (2 * (h % 2) + h // 2) * 65
                                    ins = T(bk[f"ml_own{d}"][:, o:o + 65], sP[d][:, h], va[b][:, h],
                                            start=True, stop=True)
                                bk.done(ins, f"ml_own{d}")
                        if v == 2:
                            pe.wait_ge(s["ss_sc"], n * 2 + 2)
                            pe.wait_ge(s["xd_ready"], n + 1)
                            bk.take(pe, "ss_past", n)
                            for d in range(2):
                                St = S[b] if d == 0 else sB[b]
                                for g in range(2):
                                    ins = T(bk["ss_past"][:, d * 256 + g * P:d * 256 + (g + 1) * P], bcT[:, 2 + g],
                                            St[:, ST_SS + g * P:ST_SS + (g + 1) * P], start=True, stop=True)
                            bk.done(ins, "ss_past")
                            bk.take(pe, "ss_own", n)
                            for h in range(H):
                                for d in range(2):
                                    ins = T(bk["ss_own"][:, h * DH:(h + 1) * DH], L[d][:, h], xd[d][:, h * DH:(h + 1) * DH],
                                            start=(d == 0), stop=(d == 1))
                            bk.done(ins, "ss_own")
                    weights(LEVELS)
                    ss.pe_increments(pe, n, va[b], hc("hg_i"), xc[b][:, 256:512])
                    pe.wait_ge(s["A_ready"], n + 1)
                    pe.wait_ge(s["Xq_ready"], n * (LEVELS + 1) + (LEVELS + 1))
                    for x in range(2):
                        bk.take(pe, f"hg_out{x}", n)
                        for p in range(2):
                            o = bk[f"hg_out{x}"][:, p * DH:(p + 1) * DH]
                            vh = hc("hg_i", (2 * p + x) * DH, DH)
                            T(o, Aw[x][:, 0, p], vh, start=True, stop=False)
                            T(o, Aw[x][:, 1, p], vh, start=False, stop=False)
                            for d in range(2):
                                St = S[b] if d == 0 else sB[b]
                                ins = T(o, Xq[LEVELS % 2][hh(x), d, p],
                                        St[hh(x), ST_HG + p * 64:ST_HG + p * 64 + 64], start=False, stop=(d == 1))
                        bk.done(ins, f"hg_out{x}")
                    bk.wait(pe, "hg_out0", n)
                    bk.wait(pe, "hg_out1", n)
                    pe.sem_inc(s["tile_done"], 1)
        k.clear(list(s.values()) + bk.sems())


QG = 4
HM = 2 * H
DQ = 32
KSPLIT = 128


def attention_keys(k, l, c, KA, KB, va):
    nc = k.nc
    ENG = 3
    with ExitStack() as c2:
        two = lambda name, shape, dt=F32: [k.sb(c2, f"{name}{b}", shape, dt) for b in range(2)]
        qk = two("qk", [P, 2, HM, 2, 16])
        rp = two("rp", [P, 2, 16])
        rot = k.sb(c2, "rot", [P, 2, HM, 2, 16])
        t1 = k.sb(c2, "t1", [P, 2, HM, 16])
        t2 = k.sb(c2, "t2", [P, 2, HM, 16])
        r1 = k.sb(c2, "r1", [P, 2, HM, DQ])
        sKA = k.sb(c2, "sKA", [P, HM, 4, DQ], BF16)
        sKB = k.sb(c2, "sKB", [P, HM, 4, DQ], BF16)
        sQA = k.sb(c2, "sQA", [P, HM, 4, DQ], BF16)
        sQB = k.sb(c2, "sQB", [P, HM, 4, DQ], BF16)
        oQA = k.sb(c2, "oQA", [P, HM * P], BF16)
        idb = k.sb(c2, "idb", [P, P], BF16)
        s = k.sems(c2, "memsets in0 in1 v_in tile_done dve_step rotated high rest_ready mid low turn_mm qa_ready "
                       "k_copied qa_stored qb_stored turns act_step")
        NLOAD = 2
        with nc.Block() as block:
            @block.sync
            def _(sp):
                sp.sem_inc(s["tile_done"], 2 * ENG)
                sp.wait_ge(s["memsets"], 1)
                vs = k.u[:, :, OFF["da_v"]:OFF["da_v"] + 256]
                for t in range(NT):
                    sp.dma_start(va[:, t, :, 0:DH], vs[t].rearrange("p (h w) -> p h w", h=H)).then_inc(s["v_in"], 16)
                for n, t, b in tile_rounds(sp, False):
                    hold(sp, s["tile_done"], n * ENG + ENG, s["turns"])
                    sp.dma_start(qk[b][:].rearrange("p a h x f -> p (a h x f)"),
                                 k.u[t, :, OFF["da_q"]:OFF["da_q"] + 512]).then_inc(s[f"in{b}"], 16)
                    sp.dma_start(rp[b][:].rearrange("p a f -> p (a f)"), k.rope[t]).then_inc(s[f"in{b}"], 16)
                sp.wait_ge(s["v_in"], 16 * NT)

            @block.gpsimd
            def _(gp):
                gp.memset(va[:, :, :, DH:DH + 1], 1.0)
                gp.memset(sQB[:, :, 2:4], 0.0)
                gp.memset(sKB[:, :, 2:4], 0.0).then_inc(s["turns"], 1)
                gp.wait_ge(s["turns"], 1)
                gp.memset(sKB[:, :, 2, 0:3], 1.0).then_inc(s["memsets"], 1)

            @block.vector
            def _(dve):
                V = nc.vector
                st = Steps(dve, s["dve_step"])
                dve.wait_ge(s["memsets"], 1)
                st.then(V.tensor_copy(idb[:], k.ident[:]))
                for n, t, b in tile_rounds(dve, False):
                    dve.wait_ge(s["tile_done"], n * ENG + 2 * ENG)
                    dve.wait_ge(s[f"in{b}"], per_buffer(n, b, NLOAD))
                    x1, x2 = qk[b][:, :, :, 0], qk[b][:, :, :, 1]
                    cs = lambda a: rp[b][:, a].unsqueeze(1).unsqueeze(1).to_broadcast([P, 2, HM, 16])
                    V.tensor_tensor(t1[:], x1, cs(0), ALU.mult)
                    st.then(V.tensor_tensor(t2[:], x2, cs(1), ALU.mult))
                    st.then(V.tensor_tensor(rot[:, :, :, 0], t1[:], t2[:], ALU.subtract))
                    V.tensor_tensor(t1[:], x1, cs(1), ALU.mult)
                    st.then(V.tensor_tensor(t2[:], x2, cs(0), ALU.mult))
                    V.tensor_tensor(rot[:, :, :, 1], t1[:], t2[:], ALU.add).then_inc(s["rotated"], 1)
                    rf = rot[:].rearrange("p a h x f -> p a h (x f)")
                    dve.wait_ge(s["high"], n + 1)
                    st.mark(V.tensor_tensor(r1[:, 0], rf[:, 0], sQA[:, :, 0], ALU.subtract))
                    V.tensor_tensor(r1[:, 1], rf[:, 1], sKA[:, :, 0], ALU.subtract).then_inc(s["rest_ready"], 1)
                    dve.wait_ge(s["mid"], n + 1)
                    V.tensor_tensor(sQB[:, :, 0], r1[:, 0], sQA[:, :, 2], ALU.subtract)
                    V.tensor_tensor(sKA[:, :, 3], r1[:, 1], sKA[:, :, 1], ALU.subtract).then_inc(s["low"], 1)
                    dve.wait_ge(s["low"], n + 1)
                    for a, dst in ((0, KA), (1, KB)):
                        dve.wait_ge(s["turn_mm"], n * 3 + (a + 1))
                        V.tensor_copy(dst[:, :, bass.ds(t * P, P)],
                                      k.bank[a][:].bitcast(BF16).rearrange("p (h j) -> p h j", h=HM)) \
                            .then_inc(s["k_copied"], 1)
                    dve.wait_ge(s["k_copied"], n * 2 + 2)
                    dve.sem_inc(s["tile_done"], 1)
                    st.clear()

            @block.scalar
            def _(act):
                act.preload_act_table_set(TABLES)
                A = nc.scalar.activation
                act.sem_inc(s["qa_stored"], 16)
                act.sem_inc(s["qb_stored"], 16)
                act.wait_ge(s["memsets"], 1)
                for n, t, b in tile_rounds(act, False):
                    act.wait_ge(s["tile_done"], n * ENG + 2 * ENG)
                    act.wait_ge(s["rotated"], n + 1)
                    act.wait_ge(s["qb_stored"], n * 16 + 16)
                    rf = rot[:].rearrange("p a h x f -> p a h (x f)")
                    twice = lambda a: a.unsqueeze(2).to_broadcast([P, HM, 2, DQ])
                    A(sQA[:, :, 0:2], twice(rf[:, 0]), ACT.Copy)
                    A(sQA[:, :, 3], rf[:, 0], ACT.Copy)
                    A(sKA[:, :, 0:4:2], twice(rf[:, 1]), ACT.Copy)
                    A(sKB[:, :, 0], rf[:, 1], ACT.Copy).then_inc(s["high"], 1)
                    act.wait_ge(s["rest_ready"], n + 1)
                    A(sQA[:, :, 2], r1[:, 0], ACT.Copy)
                    A(sQB[:, :, 1], r1[:, 0], ACT.Copy)
                    A(sKA[:, :, 1], r1[:, 1], ACT.Copy)
                    A(sKB[:, :, 1], r1[:, 1], ACT.Copy).then_inc(s["mid"], 1)
                    act.wait_ge(s["low"], n + 1)
                    act.dma_start(k.qb[t], sQB[:].rearrange("p h a n -> p (h a n)")).then_inc(s["qb_stored"], 16)
                    act.wait_ge(s["turn_mm"], n * 3 + 3)
                    act.wait_ge(s["qa_stored"], n * 16 + 16)
                    A(oQA[:], k.bank[2][:].bitcast(BF16), ACT.Copy).then_inc(s["qa_ready"], 1)
                    act.wait_ge(s["qa_ready"], n + 1)
                    act.dma_start(k.qa[t], oQA[:]).then_inc(s["qa_stored"], 16)
                    act.sem_inc(s["tile_done"], 1)
                act.wait_ge(s["qa_stored"], 16 * (NT + 1))
                act.wait_ge(s["qb_stored"], 16 * (NT + 1))

            @block.tensor
            def _(pe):
                for n, t, b in tile_rounds(pe, False):
                    pe.wait_ge(s["tile_done"], n * ENG + 2 * ENG)
                    pe.wait_ge(s["low"], n + 1)
                    for a, src in enumerate((sKA, sKB, sQA)):
                        for h in range(HM):
                            ins = nc.tensor.transpose(k.bank[a][:].bitcast(BF16)[:, h * P:(h + 1) * P],
                                                      src[:, h].rearrange("p a n -> p (a n)"), idb[:])
                        ins.then_inc(s["turn_mm"], 1)
                    pe.wait_ge(s["turn_mm"], n * 3 + 3)
                    pe.sem_inc(s["tile_done"], 1)
        k.clear(s.values())


def attention(k, l):
    nc = k.nc
    lam_init = 0.8 - 0.6 * math.exp(-0.3 * l)
    scale = DQ ** -0.5
    with ExitStack() as c:
        KA = k.sb(c, "KA", [P, HM, NT * P], BF16)
        KB = k.sb(c, "KB", [P, HM, NT * P], BF16)
        va = k.sb(c, "va", [P, NT, H, DH + 1])
        attention_keys(k, l, c, KA, KB, va)
        k.tag += "m"
        two = lambda name, shape, dt=F32: [k.sb(c, f"{name}{b}", shape, dt) for b in range(2)]
        QA = two("QA", [P, QG, HM * P], BF16)
        QB = two("QB", [P, QG, HM * P], BF16)
        QT = two("QT", [P, QG * P], BF16)
        PT = [k.sb(c, f"PT{b}", [P, QG * P]) for b in range(3)]
        mxp = two("mxp", [P, QG, 3])
        mneg = two("mneg", [P, QG])
        mr = two("mr", [P, QG])
        rd = k.sb(c, "rd", [P, QG])
        om = two("om", [P, QG, DH])
        o = k.sb(c, "o", [P, QG, 256])
        sq = k.sb(c, "sq", [P, QG, 256])
        z = two("z", [P, QG, 256])
        ssq = k.sb(c, "ssq", [P, QG * H])
        gr = k.sb(c, "gr", [P, DH])
        lv = k.sb(c, "lv", [P, 4, DQ])
        lm = k.sb(c, "lm", [P, 4])
        eps = k.sb(c, "eps", [P, 1])
        idb = k.sb(c, "idb", [P, P], BF16)
        s = k.sems(c, "consts_in memsets in0 in1 dve_step act_step turns lam_dot lam_exp mx_mm mx_read qb_ready qt_mm "
                      "qt_copied st_mm exp_done pv_mm pv_read gp_step ssq_ready rstd_ready out_ready stored group_done ready")
        LAT = (QG, list(range(NT)), [(0, 1024), (1024, 2048), (2048, NT * P)])
        CTXG = (CT, list(range(CT)), [(0, CTX)])
        per = lambda shape: {"mx": HM * shape[0] * len(shape[2]), "hm": HM, "kt": HM * len(shape[1]), "one": 1}
        base = per(CTXG) if l == 0 else {"mx": 0, "hm": 0, "kt": 0, "one": 0}
        zero = {"mx": 0, "hm": 0, "kt": 0, "one": 0}
        NLOAD = 3

        def groups(eng):
            if l == 0:
                yield CTXG, (lambda kind, i: i), 1, 0, 0, 0
            with eng.Fori(0, (NT - CT) // (2 * QG)) as i:
                for b in range(2):
                    yield (LAT, (lambda kind, j: (i * 2) * per(LAT)[kind] + (b * per(LAT)[kind] + base[kind] + j)),
                           b, i + (1 if l == 0 and b == 1 else 0), i * (2 * QG) + (CT + b * QG), i * 2 + (b + base["one"]))

        with nc.Block() as block:
            @block.sync
            def _(sp):
                for out_, in_ in ((gr[:], k.x["da_norm_g"][l].unsqueeze(0).to_broadcast([P, DH])),
                                  (lv[:].rearrange("p a n -> p (a n)"),
                                   k.x["da_lambda"][l].rearrange("a n -> (a n)").unsqueeze(0).to_broadcast([P, 4 * DQ]))):
                    sp.dma_start(out_, in_).then_inc(s["consts_in"], 16)
                sp.sem_inc(s["group_done"], 2)
                for (nq, kts, units), cnt, b, r, t0, g in groups(sp):
                    hold(sp, s["group_done"], g + 1, s["turns"])
                    ts = bass.ds(t0, nq)
                    sp.dma_start(QA[b][:, 0:nq], k.qa[ts].rearrange("t p n -> p t n")).then_inc(s[f"in{b}"], 16)
                    sp.dma_start(QB[b][:, 0:nq], k.qb[ts].rearrange("t p n -> p t n")).then_inc(s[f"in{b}"], 16)
                    sp.dma_start(z[b][:, 0:nq], k.u[ts, :, OFF["da_z"]:OFF["da_z"] + 256].rearrange("t p n -> p t n")) \
                        .then_inc(s[f"in{b}"], 16)

            @block.gpsimd
            def _(gp):
                V = nc.gpsimd
                st = Steps(gp, s["gp_step"])
                gp.memset(eps[:], EPS).then_inc(s["memsets"], 1)
                gp.wait_ge(s["ready"], 1)
                for (nq, kts, units), cnt, b, r, t0, g in groups(gp):
                    of = lambda a: a[:, 0:nq].rearrange("p q (h w) -> p (q h) w", h=H)
                    gp.wait_ge(s[f"in{b}"], r * (16 * NLOAD) + 16 * NLOAD)
                    st.then(V.tensor_tensor(of(z[b]), of(z[b]), gr[:].unsqueeze(1).to_broadcast([P, nq * H, DH]),
                                            ALU.mult))
                    gp.wait_ge(s["rstd_ready"], cnt("one", 1))
                    st.then(V.tensor_tensor(of(o), of(o), ssq[:, 0:nq * H].unsqueeze(2).to_broadcast([P, nq * H, DH]),
                                            ALU.mult))
                    V.tensor_tensor(o[:, 0:nq], o[:, 0:nq], z[b][:, 0:nq], ALU.mult).then_inc(s["out_ready"], 1)
                    gp.wait_ge(s["out_ready"], cnt("one", 1))
                    gp.sem_inc(s["group_done"], 1)
                    st.clear()

            @block.vector
            def _(dve):
                V = nc.vector
                st = Steps(dve, s["dve_step"])
                dve.sem_inc(s["stored"], 16)
                dve.wait_ge(s["consts_in"], 32)
                dve.wait_ge(s["memsets"], 1)
                st.then(V.tensor_tensor(lv[:, 0:4:2], lv[:, 0:4:2], lv[:, 1:4:2], ALU.mult))
                V.tensor_reduce(lm[:, 0:2], lv[:, 0:4:2], AX.X, ALU.add).then_inc(s["lam_dot"], 1)
                dve.wait_ge(s["lam_exp"], 1)
                st.then(V.tensor_tensor(lm[:, 2:3], lm[:, 1:2], lm[:, 0:1], ALU.subtract))
                st.then(V.tensor_scalar(lm[:, 3:4], lm[:, 2:3], lam_init, None, ALU.subtract))
                st.then(V.tensor_scalar(gr[:], gr[:], 1.0 - lam_init, None, ALU.mult))
                V.tensor_copy(idb[:], k.ident[:]).then_inc(s["ready"], 1)
                st.clear()
                for (nq, kts, units), cnt, b, r, t0, g in groups(dve):
                    U = len(units)

                    def maxima(hm):
                        p = hm % 2
                        for j in range(nq * U):
                            q, un = j // U, j % U
                            lo, hi = units[un]
                            dve.wait_ge(s["mx_mm"], cnt("mx", hm * nq * U + j + 1))
                            pair = (hm * nq * U + j) % 2
                            ins = V.tensor_reduce(mxp[p][:, q, un:un + 1],
                                                  k.psum[:, 1024 * pair:1024 * pair + hi - lo], AX.X, ALU.max)
                            ins.then_inc(s["mx_read"], 1)
                        dve.wait_ge(s["mx_read"], cnt("mx", (hm + 1) * nq * U))
                        st.then(V.tensor_reduce(mneg[p][:, 0:nq], mxp[p][:, 0:nq, 0:U], AX.X, ALU.max, negate=True))
                        if hm == 0:
                            dve.wait_ge(s[f"in{b}"], r * (16 * NLOAD) + 16 * NLOAD)
                        part = lambda i: QB[b][:, 0:nq, hm * P + 2 * DQ + i]
                        st.then(V.tensor_copy(part(0), mneg[p][:, 0:nq]))
                        st.then(V.tensor_tensor(mr[p][:, 0:nq], mneg[p][:, 0:nq], part(0), ALU.subtract))
                        st.then(V.tensor_copy(part(1), mr[p][:, 0:nq]))
                        V.tensor_tensor(part(2), mr[p][:, 0:nq], part(1), ALU.subtract).then_inc(s["qb_ready"], 1)

                    def outputs(hm):
                        h, m = hm // 2, hm % 2
                        dve.wait_ge(s["pv_mm"], cnt("kt", (hm + 1) * len(kts)))
                        acc = k.bank[6][:, 0:nq * 65].rearrange("p (q w) -> p q w", q=nq)
                        st.then(V.reciprocal(rd[:, 0:nq], acc[:, :, DH]))
                        if m:
                            st.then(V.tensor_scalar(rd[:, 0:nq], rd[:, 0:nq], lm[:, 3:4], None, ALU.mult))
                        elif h == 0:
                            dve.wait_ge(s["stored"], cnt("one", 1) * 16)
                        out_ = om[0] if m else om[1]
                        st.then(V.tensor_tensor(out_[:, 0:nq], acc[:, :, 0:DH],
                                                rd[:, 0:nq].unsqueeze(2).to_broadcast([P, nq, DH]), ALU.mult))
                        dve.sem_inc(s["pv_read"], 1)
                        if m:
                            st.then(V.tensor_tensor(o[:, 0:nq, h * DH:(h + 1) * DH], om[0][:, 0:nq], om[1][:, 0:nq], ALU.add))

                    maxima(0)
                    of = lambda a: a[:, 0:nq].rearrange("p q (h w) -> p (q h) w", h=H)
                    for hm in range(HM):
                        if hm + 1 < HM:
                            maxima(hm + 1)
                        outputs(hm)
                    st.then(V.tensor_tensor(sq[:, 0:nq], o[:, 0:nq], o[:, 0:nq], ALU.mult))
                    V.tensor_reduce(ssq[:, 0:nq * H], sq[:, 0:nq].rearrange("p q (h w) -> p (q h) w", h=H), AX.X, ALU.add) \
                        .then_inc(s["ssq_ready"], 1)
                    st.clear()

            @block.scalar
            def _(act):
                act.preload_act_table_set(TABLES)
                A = nc.scalar.activation
                act.wait_ge(s["lam_dot"], 1)
                A(lm[:, 0:2], lm[:, 0:2], ACT.Exp).then_inc(s["lam_exp"], 1)
                st = Steps(act, s["act_step"])
                act.wait_ge(s["memsets"], 1)
                for (nq, kts, units), cnt, b, r, t0, g in groups(act):
                    w = nq * P
                    NK = len(kts)

                    def turned(hm):
                        act.wait_ge(s["qt_mm"], cnt("hm", hm + 1))
                        A(QT[hm % 2][:, 0:w], k.bank[7][:].bitcast(BF16)[:, 0:w], ACT.Copy).then_inc(s["qt_copied"], 1)

                    turned(0)
                    for hm in range(HM):
                        for i in range(NK):
                            j = hm * NK + i
                            if i == NK - 1 and hm + 1 < HM:
                                turned(hm + 1)
                            act.wait_ge(s["st_mm"], cnt("kt", j + 1))
                            A(PT[j % 3][:, 0:w], k.bank[4 + j % 2][:, 0:w], ACT.Exp, scale=scale) \
                                .then_inc(s["exp_done"], 1)
                    act.wait_ge(s["ssq_ready"], cnt("one", 1))
                    st.then(A(ssq[:, 0:nq * H], ssq[:, 0:nq * H], ACT.Ln, scale=1.0 / DH, bias=eps[:]))
                    A(ssq[:, 0:nq * H], ssq[:, 0:nq * H], ACT.Exp, scale=-0.5).then_inc(s["rstd_ready"], 1)
                    act.wait_ge(s["out_ready"], cnt("one", 1))
                    act.dma_start(k.y[bass.ds(t0, nq), :, 256:512].rearrange("t p n -> p t n"), o[:, 0:nq]) \
                        .then_inc(s["stored"], 16)
                    st.clear()
                act.wait_ge(s["stored"], 16 * ((NT - CT) // QG + base["one"] + 1))

            @block.tensor
            def _(pe):
                T = nc.tensor.matmul
                pe.wait_ge(s["ready"], 1)
                for (nq, kts, units), cnt, b, r, t0, g in groups(pe):
                    w = nq * P
                    U = len(units)
                    NK = len(kts)
                    first = []

                    def unit(hm, j):
                        q, (lo, hi) = j // U, units[j % U]
                        x = hm * nq * U + j
                        if x >= 2:
                            pe.wait_ge(s["mx_read"], cnt("mx", x - 1))
                        for a in range(lo, hi, 512):
                            e = min(a + 512, hi)
                            ins = T(k.psum[:, 1024 * (x % 2) + a - lo:1024 * (x % 2) + e - lo],
                                    QA[b][:, q, hm * P:(hm + 1) * P], KA[:, hm, a:e], start=True, stop=True)
                        ins.then_inc(s["mx_mm"], 1)

                    def turn(hm):
                        pe.wait_ge(s["qb_ready"], cnt("hm", hm + 1))
                        if hm:
                            pe.wait_ge(s["qt_copied"], cnt("hm", hm))
                        for q in range(nq):
                            ins = nc.tensor.transpose(k.bank[7][:].bitcast(BF16)[:, q * P:(q + 1) * P],
                                                      QB[b][:, q, hm * P:(hm + 1) * P], idb[:])
                        ins.then_inc(s["qt_mm"], 1)

                    def scores(hm, i):
                        j = hm * NK + i
                        if i == 0:
                            pe.wait_ge(s["qt_copied"], cnt("hm", hm + 1))
                        kt = kts[i]
                        T(k.bank[4 + j % 2][:, 0:w], KA[:, hm, kt * P:(kt + 1) * P],
                          QA[b][:, 0:nq, hm * P:(hm + 1) * P], start=True, stop=False)
                        T(k.bank[4 + j % 2][:, 0:w], KB[:, hm, kt * P:(kt + 1) * P], QT[hm % 2][:, 0:w],
                          start=False, stop=True).then_inc(s["st_mm"], 1)

                    def values(j):
                        hm, i = j // NK, j % NK
                        pe.wait_ge(s["exp_done"], cnt("kt", j + 1))
                        if i == 0 and hm:
                            pe.wait_ge(s["pv_read"], cnt("hm", hm))
                        for q in range(nq):
                            ins = T(k.bank[6][:, q * 65:(q + 1) * 65], PT[j % 3][:, q * P:(q + 1) * P],
                                    va[:, kts[i], hm // 2], start=(i == 0 and q == 0), stop=(i == NK - 1),
                                    skip_group_check=True)
                        ins.then_inc(s["pv_mm"], 1)

                    pe.wait_ge(s[f"in{b}"], r * (16 * NLOAD) + 16 * NLOAD)
                    for j in range(nq * U):
                        unit(0, j)
                    turn(0)
                    for hm in range(HM):
                        todo = list(range(nq * U)) if hm + 1 < HM else []
                        for i in range(NK):
                            if i == NK - 1 and hm + 1 < HM:
                                for j in todo:
                                    unit(hm + 1, j)
                                todo = []
                                turn(hm + 1)
                            scores(hm, i)
                            if todo:
                                unit(hm + 1, todo.pop(0))
                            j = hm * NK + i
                            if j >= 1:
                                values(j - 1)
                    values(HM * NK - 1)
        k.clear(s.values())


def output(k, l):
    nc = k.nc
    last = l == DEPTH - 1
    ENG = 3
    with ExitStack() as c:
        two = lambda name, shape: [k.sb(c, f"{name}{b}", shape) for b in range(2)]
        W = k.sb(c, "W", [P, KT, D])
        y = two("y", [P, D])
        x = two("x", [P, D])
        yT = two("yT", [P, KT, P])
        o = two("o", [P, D])
        gate = k.sb(c, "gate", [P, 2, D])
        fg = k.sb(c, "fg", [P, D])
        eps = k.sb(c, "eps", [P, 1])
        sm = k.sb(c, "sm", [P, 4])
        s = k.sems(c, "consts_in in0 in1 tile_done turn_mm turn_copied out_mm summed normed stored0 stored1 turns "
                      "act_step dve_step memsets")
        xc_, xl = layer_input(k, l)
        loops = (((0, 1, 1),) if not last else ()) + ((CT if not last else 0, (NT - CT) // 2, 0),)

        def rounds(eng):
            for first, n, kind in loops:
                with eng.Fori(0, n) as i:
                    for b in range(2):
                        yield i * 2 + (first + b), b, i * 2 + ((0 if kind else CT) + b), i * 2 + b, kind

        with nc.Block() as block:
            @block.sync
            def _(sp):
                sp.sem_inc(s["tile_done"], 2 * ENG)
                wv = k.x["w_out"][l].rearrange("(k p) n -> p k n", p=P)
                sp.dma_start(W[:], wv).then_inc(s["consts_in"], 16)
                for a in range(2):
                    sp.dma_start(gate[:, a], k.modrow[l, a, 2 * D:3 * D].unsqueeze(0).to_broadcast([P, D])) \
                        .then_inc(s["consts_in"], 16)
                sp.dma_start(fg[:], k.x["final_g"].unsqueeze(0).to_broadcast([P, D])).then_inc(s["consts_in"], 16)
                for n, b, t, ti, kind in rounds(sp):
                    hold(sp, s["tile_done"], n * ENG + ENG, s["turns"])
                    sp.dma_start(y[b][:], k.y[t]).then_inc(s[f"in{b}"], 16)
                    sp.dma_start(x[b][:], (xc_ if kind else xl)[ti]).then_inc(s[f"in{b}"], 16)

            @block.gpsimd
            def _(gp):
                gp.memset(eps[:], EPS).then_inc(s["memsets"], 1)

            @block.tensor
            def _(pe):
                pe.wait_ge(s["consts_in"], 64)
                for n, b, t, ti, kind in rounds(pe):
                    pe.wait_ge(s["tile_done"], n * ENG + 2 * ENG)
                    pe.wait_ge(s[f"in{b}"], per_buffer(n, b, 2))
                    for q in range(KT):
                        ins = nc.tensor.transpose(k.bank[q // 4][:, (q % 4) * P:(q % 4 + 1) * P],
                                                  y[b][:, q * P:(q + 1) * P], k.ident[:])
                    ins.then_inc(s["turn_mm"], 1)
                    pe.wait_ge(s["turn_copied"], n + 1)
                    for a in range(2):
                        for q in range(KT):
                            ins = nc.tensor.matmul(k.bank[2 + a][:], yT[b][:, q], W[:, q, a * 512:(a + 1) * 512],
                                                   start=(q == 0), stop=(q == KT - 1))
                        ins.then_inc(s["out_mm"], 1)
                    pe.wait_ge(s["out_mm"], n * 2 + 2)
                    pe.sem_inc(s["tile_done"], 1)

            @block.vector
            def _(dve):
                V = nc.vector
                st = Steps(dve, s["dve_step"])
                dve.wait_ge(s["consts_in"], 64)
                for n, b, t, ti, kind in rounds(dve):
                    dve.wait_ge(s["tile_done"], n * ENG + 2 * ENG)
                    dve.wait_ge(s[f"in{b}"], per_buffer(n, b, 2))
                    dve.wait_ge(s[f"stored{b}"], per_buffer(n, b, 1))
                    for a in range(2):
                        dve.wait_ge(s["out_mm"], n * 2 + (a + 1))
                        sl = slice(a * 512, (a + 1) * 512)
                        st.then(V.tensor_tensor(o[b][:, sl], k.bank[2 + a][:], gate[:, kind, sl], ALU.mult))
                    V.tensor_tensor(o[b][:], o[b][:], x[b][:], ALU.add).then_inc(s["summed"], 1)
                    dve.wait_ge(s["summed"], n * (1 + last) + 1)
                    if last:
                        dve.wait_ge(s["normed"], n + 1)
                        V.scalar_tensor_tensor(o[b][:], o[b][:], sm[:, 2:3], fg[:], ALU.mult, ALU.mult) \
                            .then_inc(s["summed"], 1)
                        dve.wait_ge(s["summed"], n * 2 + 2)
                    dve.sem_inc(s["tile_done"], 1)
                    st.clear()

            @block.scalar
            def _(act):
                act.preload_act_table_set(TABLES)
                A = nc.scalar.activation
                st = Steps(act, s["act_step"])
                for b in range(2):
                    act.sem_inc(s[f"stored{b}"], 16)
                act.wait_ge(s["memsets"], 1)
                for n, b, t, ti, kind in rounds(act):
                    act.wait_ge(s["tile_done"], n * ENG + 2 * ENG)
                    act.wait_ge(s["turn_mm"], n + 1)
                    for a in range(2):
                        ins = A(yT[b][:, 4 * a:4 * a + 4].rearrange("p q n -> p (q n)"), k.bank[a][:], ACT.Copy)
                    ins.then_inc(s["turn_copied"], 1)
                    act.wait_ge(s["turn_copied"], n + 1)
                    act.wait_ge(s["summed"], n * (1 + last) + 1)
                    if last:
                        st.then(A(y[b][:], o[b][:], ACT.Square, accum_out=sm[:, 0:1]))
                        st.then(A(sm[:, 1:2], sm[:, 0:1], ACT.Ln, scale=1.0 / D, bias=eps[:]))
                        A(sm[:, 2:3], sm[:, 1:2], ACT.Exp, scale=-0.5).then_inc(s["normed"], 1)
                        act.wait_ge(s["summed"], n * 2 + 2)
                        act.dma_start(k.out[0].rearrange("(t p) n -> t p n", p=P)[ti], o[b][:]) \
                            .then_inc(s[f"stored{b}"], 16)
                    else:
                        act.dma_start(k.stream[t], o[b][:]).then_inc(s[f"stored{b}"], 16)
                    act.sem_inc(s["tile_done"], 1)
                    st.clear() if last else None
                for b in range(2):
                    act.wait_ge(s[f"stored{b}"], 16 * ((NT - CT * last) // 2 + 1))
        k.clear(s.values())


IN_NAMES = ["x", "c", "ctx", "c_ctx", "w_mod", "b_mod", "norm_g", "w_in", "w_out", "ml_gate_b", "ml_norm_g",
            "da_lambda", "da_norm_g", "ss_conv_w", "ss_conv_b", "ss_dt_bias", "ss_a_log", "ss_d", "ss_norm_g",
            "hg_lower", "hg_norm_g", "final_g"]


def build(nc, ins, out, phases=None, preset=()):
    k = Kernel(nc, ins, out, preset)
    with ExitStack() as c:
        k.psum = c.enter_context(nc.psum_tensor("psum", [P, BANKS * 512], F32))
        k.bank = [k.psum[:, 512 * i:512 * (i + 1)] for i in range(BANKS)]
        k.ident = k.sb(c, "ident", [P, P])
        k.mod = k.sb(c, "mod", [P, DEPTH, 24, 2])
        k.loaded_before = 0
        k.queue_sems = k.sems(c, "x_in0 x_in1")
        load = k.sem(c, "const_in")
        nc.sync.dma_start(k.ident[:], ins["c_ident"]).then_inc(load, 16)
        nc.sync.wait_ge(load, 16)
        nc.all_engine_barrier()
        todo = [("modulation", modulation, ())]
        for l in range(DEPTH):
            todo.append((f"projection{l}", projection, (l,)))
            todo.append((f"gates{l}", gates, (l,)))
            todo.append((f"states{l}", states, (l,)))
            todo.append((f"mixing{l}", mixing, (l,)))
            todo.append((f"attention{l}", attention, (l,)))
            todo.append((f"output{l}", output, (l,)))
        c.enter_context(nc.allow_non_contiguous_dma(reason="short parameter vectors turned into columns"))
        for name, f, args in todo:
            if phases is None or name in phases:
                k.tag = name
                f(k, *args)


def kernel(**inputs):
    import concourse.bacc as _bacc
    from concourse.bass_utils import run_bass_kernel_spmd as _run

    nc = _bacc.Bacc("TRN2", target_bir_lowering=False, num_devices=1)
    arrays, ins = {}, {}
    for name, a in [(n, np.ascontiguousarray(inputs[n])) for n in IN_NAMES] + list(dram_constants().items()):
        arrays[f"in_{name}"] = a
        ins[name] = nc.dram_tensor(f"in_{name}", a.shape, mybir.dt.from_np(a.dtype), kind="ExternalInput").ap()
    out = nc.dram_tensor("out", (1, SEQ, D), F32, kind="ExternalOutput").ap()
    build(nc, ins, out)
    r = _run(nc, [arrays], core_ids=[0])
    return r.results[0]["out"]
```
